# Optimizing a Trainium2 kernel written in Bass

```python
import math
import jax, jax.numpy as jnp
from jax import lax
import numpy as np

D_MODEL = 1024
BATCH = 1
SEQ = 1024
DEPTH = 1

CHUNK = 64
Q_BLOCK = 128

MLA_HEADS = 8
QK_NOPE_DIM = 64
QK_ROPE_DIM = 32
QK_HEAD_DIM = QK_NOPE_DIM + QK_ROPE_DIM
V_HEAD_DIM = 64
MLA_WIDTH = MLA_HEADS * V_HEAD_DIM
Q_LORA_RANK = 256
KV_LORA_RANK = 128
ROPE_THETA = 10000.0

RNN_WIDTH = 512
RNN_BLOCKS = 8
RNN_BLOCK_DIM = RNN_WIDTH // RNN_BLOCKS
CONV_WIDTH = 4
LRU_C = 8.0

MIX_WIDTH = MLA_WIDTH + RNN_WIDTH

IN_SPLITS = (Q_LORA_RANK, KV_LORA_RANK, QK_ROPE_DIM, MLA_WIDTH, RNN_WIDTH, RNN_WIDTH)
IN_WIDTH = sum(IN_SPLITS)

NORM_EPS = 1e-6

kernel_name = "hymba_mla_rglru_chunk_causal"

def rmsnorm(x, g):
    xf = x.astype(jnp.float32)
    y = xf * lax.rsqrt(jnp.mean(xf * xf, axis=-1, keepdims=True) + NORM_EPS)
    return (y * g.astype(jnp.float32)).astype(x.dtype)

def rope_tables(seq):
    pos = jnp.arange(seq, dtype=jnp.float32)
    inv_freq = ROPE_THETA ** (-jnp.arange(0, QK_ROPE_DIM, 2, dtype=jnp.float32) / QK_ROPE_DIM)
    ang = pos[:, None] * inv_freq[None, :]
    return jnp.cos(ang), jnp.sin(ang)

def apply_rope(x, cos, sin):
    xf = x.astype(jnp.float32)
    x1, x2 = jnp.split(xf, 2, axis=-1)
    out = jnp.concatenate([x1 * cos - x2 * sin, x2 * cos + x1 * sin], axis=-1)
    return out.astype(x.dtype)

def chunk_causal_attention(q, k, v):
    b, s, h, dqk = q.shape
    nqb = s // Q_BLOCK
    scale = 1.0 / math.sqrt(QK_HEAD_DIM)
    qb = q.reshape(b, nqb, Q_BLOCK, h, dqk).transpose(1, 0, 2, 3, 4)
    kf = k.astype(jnp.float32)
    key_chunk = jnp.arange(s) // CHUNK

    def one_block(args):
        q_blk, bi = args
        q_pos = bi * Q_BLOCK + jnp.arange(Q_BLOCK)
        sc = jnp.einsum('bqhd,bkhd->bhqk', q_blk.astype(jnp.float32), kf) * scale
        mask = key_chunk[None, :] <= (q_pos // CHUNK)[:, None]
        sc = jnp.where(mask[None, None], sc, jnp.finfo(jnp.float32).min)
        p = jax.nn.softmax(sc, axis=-1)
        return jnp.einsum('bhqk,bkhd->bqhd', p.astype(v.dtype), v)

    out = lax.map(one_block, (qb, jnp.arange(nqb)))
    return out.transpose(1, 0, 2, 3, 4).reshape(b, s, h * v.shape[-1])

def causal_depthwise_conv(x, w, bias):
    c = x.shape[-1]
    y = lax.conv_general_dilated(
        x, w[:, None, :].astype(x.dtype), window_strides=(1,),
        padding=((CONV_WIDTH - 1, 0),), dimension_numbers=('NWC', 'WIO', 'NWC'),
        feature_group_count=c)
    return y + bias.astype(x.dtype)

def rg_lru(x, w_a, b_a, w_x, b_x, lru_param):
    b, s, _ = x.shape
    xf = x.astype(jnp.float32)
    xb = xf.reshape(b, s, RNN_BLOCKS, RNN_BLOCK_DIM)
    r = jax.nn.sigmoid(jnp.einsum('bsnc,ncd->bsnd', xb, w_a.astype(jnp.float32)).reshape(b, s, -1)
                       + b_a.astype(jnp.float32))
    i = jax.nn.sigmoid(jnp.einsum('bsnc,ncd->bsnd', xb, w_x.astype(jnp.float32)).reshape(b, s, -1)
                       + b_x.astype(jnp.float32))
    log_a = -LRU_C * r * jax.nn.softplus(-lru_param.astype(jnp.float32))
    a = jnp.exp(log_a)
    mult = jnp.sqrt(jnp.clip(1.0 - jnp.exp(2.0 * log_a), 1e-12, None))
    is_start = (jnp.arange(s) == 0)[None, :, None]
    mult = jnp.where(is_start, 1.0, mult)
    u = mult * (i * xf)

    def combine(left, right):
        a_l, h_l = left
        a_r, h_r = right
        return a_l * a_r, a_r * h_l + h_r

    _, h = lax.associative_scan(combine, (a, u), axis=1)
    return h.astype(x.dtype)

def setup_inputs(seed: int = 0) -> dict:
    key = jax.random.key(seed)
    ks = jax.random.split(key, 20)
    f32 = jnp.float32

    def w(k, shape, fan_in):
        return jax.random.normal(k, shape, f32) * (fan_in ** -0.5)

    def gain(k, shape):
        return 1.0 + 0.05 * jax.random.normal(k, shape, f32)

    def bias(k, shape):
        return 0.01 * jax.random.normal(k, shape, f32)

    u = jax.random.uniform(ks[13], (DEPTH, RNN_WIDTH), f32, 0.9, 0.999)
    base = u ** (1.0 / LRU_C)
    lru_param = jnp.log(base) - jnp.log1p(-base)

    return {
        "x": jax.random.normal(ks[0], (BATCH, SEQ, D_MODEL), f32),
        "norm_in_g": gain(ks[1], (DEPTH, D_MODEL)),
        "w_in": w(ks[2], (DEPTH, D_MODEL, IN_WIDTH), D_MODEL),
        "q_norm_g": gain(ks[3], (DEPTH, Q_LORA_RANK)),
        "w_q_b": w(ks[4], (DEPTH, Q_LORA_RANK, MLA_HEADS * QK_HEAD_DIM), Q_LORA_RANK),
        "kv_norm_g": gain(ks[5], (DEPTH, KV_LORA_RANK)),
        "w_kv_b": w(ks[6], (DEPTH, KV_LORA_RANK, MLA_HEADS * (QK_NOPE_DIM + V_HEAD_DIM)), KV_LORA_RANK),
        "conv_w": w(ks[7], (DEPTH, CONV_WIDTH, RNN_WIDTH), CONV_WIDTH),
        "conv_b": bias(ks[8], (DEPTH, RNN_WIDTH)),
        "w_rg_a": w(ks[9], (DEPTH, RNN_BLOCKS, RNN_BLOCK_DIM, RNN_BLOCK_DIM), RNN_BLOCK_DIM),
        "b_rg_a": bias(ks[10], (DEPTH, RNN_WIDTH)),
        "w_rg_x": w(ks[11], (DEPTH, RNN_BLOCKS, RNN_BLOCK_DIM, RNN_BLOCK_DIM), RNN_BLOCK_DIM),
        "b_rg_x": bias(ks[12], (DEPTH, RNN_WIDTH)),
        "lru_param": lru_param,
        "out_norm_mla_g": gain(ks[14], (DEPTH, MLA_WIDTH)),
        "out_norm_rnn_g": gain(ks[15], (DEPTH, RNN_WIDTH)),
        "w_out": w(ks[16], (DEPTH, MIX_WIDTH, D_MODEL), MIX_WIDTH),
        "final_norm_g": gain(ks[17], (D_MODEL,)),
    }

def reference(x, norm_in_g, w_in, q_norm_g, w_q_b, kv_norm_g, w_kv_b, conv_w, conv_b,
              w_rg_a, b_rg_a, w_rg_x, b_rg_x, lru_param, out_norm_mla_g, out_norm_rnn_g,
              w_out, final_norm_g):
    b, s, _ = x.shape
    cos, sin = rope_tables(s)
    offs = np.cumsum(IN_SPLITS)[:-1].tolist()

    for l in range(DEPTH):
        h = rmsnorm(x, norm_in_g[l])
        z = jnp.einsum('bsd,de->bse', h, w_in[l])
        q_lat, kv_lat, k_rope, g_mla, x_rnn, g_rnn = jnp.split(z, offs, axis=-1)

        q = jnp.einsum('bsr,re->bse', rmsnorm(q_lat, q_norm_g[l]), w_q_b[l])
        q = q.reshape(b, s, MLA_HEADS, QK_HEAD_DIM)
        q_nope, q_pe = q[..., :QK_NOPE_DIM], q[..., QK_NOPE_DIM:]
        q_pe = apply_rope(q_pe, cos[:, None, :], sin[:, None, :])
        kv = jnp.einsum('bsr,re->bse', rmsnorm(kv_lat, kv_norm_g[l]), w_kv_b[l])
        kv = kv.reshape(b, s, MLA_HEADS, QK_NOPE_DIM + V_HEAD_DIM)
        k_nope, v = kv[..., :QK_NOPE_DIM], kv[..., QK_NOPE_DIM:]
        k_pe = apply_rope(k_rope, cos, sin)
        k_pe = jnp.broadcast_to(k_pe[:, :, None, :], (b, s, MLA_HEADS, QK_ROPE_DIM))
        q_full = jnp.concatenate([q_nope, q_pe], axis=-1)
        k_full = jnp.concatenate([k_nope, k_pe], axis=-1)
        y_mla = chunk_causal_attention(q_full, k_full, v)

        xr = causal_depthwise_conv(x_rnn, conv_w[l], conv_b[l])
        y_rnn = rg_lru(xr, w_rg_a[l], b_rg_a[l], w_rg_x[l], b_rg_x[l], lru_param[l])

        y_mla = rmsnorm(y_mla, out_norm_mla_g[l]) * jax.nn.silu(g_mla)
        y_rnn = rmsnorm(y_rnn, out_norm_rnn_g[l]) * jax.nn.silu(g_rnn)
        y = jnp.concatenate([y_mla, y_rnn], axis=-1)
        x = x + jnp.einsum('bse,ed->bsd', y, w_out[l])

    return rmsnorm(x, final_norm_g)


_drawn_inputs = setup_inputs


def setup_inputs(seed=0):
    import zlib

    import numpy as np

    out = dict(_drawn_inputs(seed))
    spreads = {}
    factors = {'q_norm_g': 3.41,
     'b_rg_a': 42.146,
     'b_rg_x': 34.144,
     'out_norm_mla_g': 3.356,
     'out_norm_rnn_g': 3.01}
    for name, (base, spread) in spreads.items():
        noise = np.random.default_rng([zlib.crc32(name.encode()), seed]).standard_normal(out[name].shape)
        drawn = base * np.exp(spread * noise) if base else spread * noise
        out[name] = __import__('jax').numpy.asarray(drawn.astype(out[name].dtype))
    for name, factor in factors.items():
        out[name] = (out[name] * factor).astype(out[name].dtype)
    return out
```

```python
import concourse.bass as bass
from concourse import mybir

F32 = mybir.dt.float32
F32R = mybir.dt.float32r
BF16 = mybir.dt.bfloat16
ALU = mybir.AluOpType
ACT = mybir.ActivationFunctionType
AX = mybir.AxisListType

P = 128
SEQ, D = 1024, 1024
NT = SEQ // P
KD = D // P
HALF = 512
H, NOPE, ROPE, VD = 8, 64, 32, 64
QK = NOPE + ROPE
QR, KVR = 256, 128
LAT = QR + KVR + ROPE
RNN = 512
NC = RNN // P
EPS = 1e-6
SCALE = float(QK) ** -0.5
MASKED = -2.0 ** 127

COL_GM, COL_X, COL_GR = LAT, LAT + RNN, LAT + 2 * RNN
CHUNKS = [("x", c, COL_X + P * c) for c in range(NC)] + \
         [("gr", c, COL_GR + P * c) for c in range(NC)] + \
         [("gm", c, COL_GM + P * c) for c in range(NC)]


def attention_steps():
    steps = [("Q", 0, 0), ("K", 0, 0), ("Q", 0, 1), ("K", 0, 1), ("V", 0, 0)]
    for t in range(3):
        steps += [("S", 0, t), ("V", 0, t + 1)]
    steps += [("S", 0, t) for t in range(3, 6)]
    for h in range(H):
        n = 2 * h
        first, second = [[] for _ in range(4)], [[] for _ in range(8)]
        first[0] += [("S", h, 6)]
        if h:
            first[1] += [("C", n - 1)]
        first[1] += [("S", h, 7)]
        second[1] += [("C", n)]
        if h + 1 < H:
            first[2] += [("Q", h + 1, 0)]
            first[3] += [("Q", h + 1, 1)]
            for t, j in enumerate((3, 4, 4, 5, 6, 7)):
                second[j] += [("S", h + 1, t)]
        if h % 2 == 0 and h + 2 < H:
            second[0] += [("K", h // 2 + 1, 0)]
            second[2] += [("K", h // 2 + 1, 1)]
        if h == 3:
            for p in range(3):
                second[2 * p + 2] += [("V", 1, p)]
        if h == 4:
            first[0] += [("V", 1, 3)]
        for item, between in ((n, first), (n + 1, second)):
            keys = len(between)
            steps += [("T", item, 0)]
            for j in range(keys):
                if j + 1 < keys:
                    steps += [("T", item, j + 1)]
                steps += between[j]
                steps += [("PV", item, j)]
            steps += [("Y", item)]
    return steps + [("C", 2 * H - 1)]


def scores_after_transposes(steps):
    start = steps.index(("T", 0, 0))
    order, held = steps[:start], []
    for step in steps[start:]:
        if step[0] == "S":
            held += [step]
        else:
            order += [step]
            if step[0] == "T":
                order += held
                held = []
    return order + held


def build(nc, a, out):
    KB = 1024
    base = (nc.sbuf_base + 31) // 32 * 32

    def at(name, shape, off, dt=F32):
        return nc.alloc_sbuf_tensor_at(name, shape, dt, offset=base + int(off))

    off = [0]

    def small(name, shape, dt=F32):
        n = 4 if dt != BF16 else 2
        for s in shape[1:]:
            n *= s
        t = at(name, shape, off[0], dt)
        off[0] += (n + 31) // 32 * 32
        return t

    trig = small("trig", [P, SEQ])
    ident = small("ident", [P, P])
    stack = small("stack", [P, VD])
    one_col = small("one_col", [P, 1])
    half_rows = small("half_rows", [1, P], BF16)
    masked = small("masked", [1, VD], BF16)
    g_mla = small("g_mla", [P, NC])
    g_rnn = small("g_rnn", [P, NC])
    conv_w = small("conv_w", [P, 4, NC])
    conv_b = small("conv_b", [P, NC])
    bias_a = small("bias_a", [P, NC])
    bias_x = small("bias_x", [P, NC])
    lru = small("lru", [P, NC])
    sp = small("sp", [P, 12, NC])
    sp8 = small("sp8", [P, NC])
    sp16 = small("sp16", [P, NC])
    inv_n = small("inv_n", [P, 2])
    minus_half = small("minus_half", [P, NT])
    ssq_x = small("ssq_x", [P, NT])
    rstd_x = small("rstd_x", [P, NT])
    ssq_z = small("ssq_z", [P, NT, 2])
    rstd_z = small("rstd_z", [P, NT, 2])
    ssq_r = small("ssq_r", [P, NT])
    rstd_r = small("rstd_r", [P, NT])
    ssq_m = small("ssq_m", [P, NT])
    rstd_m = small("rstd_m", [P, NT])
    ssq_o = small("ssq_o", [P, NT])
    rstd_o = small("rstd_o", [P, NT])
    nmax = small("nmax", [P, H * NT])
    bias_s = small("bias_s", [P, H * NT])
    rsum = small("rsum", [P, H * NT])
    rinv = small("rinv", [P, H * NT])
    assert off[0] <= 7.5 * KB, off[0]
    B0 = 7.5 * KB
    latT_h = at("latT_h", [P, 3, SEQ], B0, F32R)
    latT_l = at("latT_l", [P, 3, SEQ], B0 + 12 * KB, F32R)
    gmT = at("gmT", [P, NC, SEQ], B0 + 24 * KB)
    yrT = at("yrT", [P, NC, SEQ], B0 + 40 * KB)
    raw = [at(f"raw{i}", [P, 1024], B0 + (56 + 4 * i) * KB) for i in range(2)]
    R1 = B0 + 64 * KB
    R2 = R1 + 50.5 * KB
    lat_w_h = at("lat_w_h", [P, KD, LAT], R1, F32R)
    lat_w_l = at("lat_w_l", [P, KD, LAT], R1 + 13 * KB, F32R)
    xst = [at(f"xst{i}", [P, D], R1 + (26 + 4 * i) * KB) for i in range(3)]
    g_in_row = at("g_in_row", [P, D], R1 + 38 * KB)
    g_lat_row = at("g_lat_row", [P, QR + KVR], R1 + 42 * KB)
    latn = [at(f"latn{i}", [P, QR + KVR], R1 + (43.5 + 1.5 * i) * KB) for i in range(2)]
    krs = [at(f"krs{i}", [P, P], R1 + (46.5 + 0.5 * i) * KB) for i in range(2)]
    rope_t = at("rope_t", [P, P], R1 + 47.5 * KB)
    hT_h = at("hT_h", [P, KD, SEQ], R2, F32R)
    hT_l = at("hT_l", [P, KD, SEQ], R2 + 32 * KB, F32R)
    cw_h = [at(f"cw_h{i}", [P, KD, P], R2 + (64 + 4 * i) * KB, F32R) for i in range(2)]
    cw_l = [at(f"cw_l{i}", [P, KD, P], R2 + (72 + 4 * i) * KB, F32R) for i in range(2)]
    kpe = at("kpe", [P, SEQ], R2 + 80 * KB)
    junk = [gmT[:, c, :] for c in (0, 2, 3)]
    gate_raw = gmT[:, 1:2, :].rearrange("p a (g c n) -> p (a g) c n", g=2, c=NC)
    xr = [gmT[:, c, :] for c in range(NC)]
    hsq = at("hsq", [P, SEQ], R1)
    xr_h = at("xr_h", [P, SEQ], R1 + 8 * KB, F32R)
    xr_l = at("xr_l", [P, SEQ], R1 + 12 * KB, F32R)
    ra = at("ra", [P, SEQ], R1 + 16 * KB)
    iu = at("iu", [P, SEQ], R1 + 20 * KB)
    mh = at("mh", [P, SEQ], R1 + 24 * KB)
    gw_h = at("gw_h", [P, 2, NC, P], R1 + 28 * KB, F32R)
    gw_l = at("gw_l", [P, 2, NC, P], R1 + 32 * KB, F32R)
    xpad = at("xpad", [P, SEQ + 4], R1 + 36 * KB)
    sg = [at(f"sg{i}", [P, HALF], R1 + (40.25 + 2 * i) * KB) for i in range(2)]
    sq_sum = at("sq_sum", [P, SEQ], R1 + 44.25 * KB)
    wq_h = at("wq_h", [P, 2, H, P], R1, F32R)
    wq_l = at("wq_l", [P, 2, H, P], R1 + 8 * KB, F32R)
    wkv_h = at("wkv_h", [P, 2 * H * VD], R1 + 16 * KB, F32R)
    wkv_l = at("wkv_l", [P, 2 * H * VD], R1 + 20 * KB, F32R)
    ynat = at("ynat", [P, NT, NC * P], R1 + 24 * KB)
    ptl = [at(f"ptl{i}", [P, HALF], R1 + (40.25 + 2 * i) * KB, F32R) for i in range(2)]
    pth = [at(f"pth{i}", [P, HALF], R1 + (44.25 + 2 * i) * KB, F32R) for i in range(2)]
    yTs = at("yTs", [P, HALF], R1 + 48.25 * KB)
    kh = at("kh", [P, 4, SEQ], R2, F32R)
    kl = at("kl", [P, 4, SEQ], R2 + 16 * KB, F32R)
    qh = at("qh", [P, SEQ], R2 + 32 * KB, F32R)
    ql = at("ql", [P, SEQ], R2 + 36 * KB, F32R)
    qt = [at(f"qt{i}", [P, HALF], R2 + (40 + 2 * i) * KB) for i in range(2)]
    vv = at("vv", [P, NT, 4, P], R2 + 44 * KB, F32R)
    probs, off[0] = {}, R2 + 60 * KB
    for t in range(NT):
        for i in range(2 if t in (4, 5) else 1):
            probs[t, i] = at(f"probs{t}_{i}", [P, P * (t + 1)], off[0])
            off[0] += 4 * P * (t + 1)
    slot4 = [B0, B0 + 4 * KB, B0 + 8 * KB, B0 + 12 * KB, R1, R1 + 4 * KB, R1 + 8 * KB, R1 + 12 * KB]
    wr_h = [at(f"wr_h{c}", [P, D], slot4[c], F32R) for c in range(NC)]
    wr_l = [at(f"wr_l{c}", [P, D], slot4[4 + c], F32R) for c in range(NC)]
    slot4 = [B0 + 16 * KB, B0 + 20 * KB, R1 + 16 * KB, R1 + 20 * KB, R2, R2 + 4 * KB, R2 + 16 * KB, R2 + 20 * KB]
    yr_h = [at(f"yr_h{c}", [P, SEQ], slot4[c], F32R) for c in range(NC)]
    yr_l = [at(f"yr_l{c}", [P, SEQ], slot4[4 + c], F32R) for c in range(NC)]
    wm_h = [at(f"wm_h{c}", [P, D], R2 + (32 + 4 * c) * KB, F32R) for c in range(NC)]
    wm_l = [at(f"wm_l{c}", [P, D], R2 + (48 + 4 * c) * KB, F32R) for c in range(NC)]
    xres = [at(f"xres{i}", [P, D], R2 + (64 + 4 * i) * KB) for i in range(4)]
    ost = [at("ost0", [P, D], R2 + 80 * KB), at("ost1", [P, D], R2 + 8 * KB)]
    fg_row = at("fg_row", [P, D], R2 + 12 * KB)
    ymf = at("ymf", [P, NC, P], R2 + 24 * KB)
    ym_h = [at(f"ym_h{i}", [P, NC, P], R2 + (26 + i) * KB + i * KB, F32R) for i in range(2)]
    ym_l = [at("ym_l0", [P, NC, P], R2 + 30 * KB, F32R), at("ym_l1", [P, NC, P], R1 + 48.25 * KB, F32R)]
    assert base + R2 + 84 * KB <= nc.sbuf_usable_end, (base, R2, nc.sbuf_usable_end)

    ps = nc.alloc_psum_tensor("ps", [P, 8, HALF], F32)

    def f32(ap):
        return ap.bitcast(F32)

    from contextlib import ExitStack
    ctx = ExitStack()

    def sem(name):
        return ctx.enter_context(nc.semaphore(name))

    first_in = sem("first_in")
    const_in = sem("const_in")
    gates_in = sem("gates_in")
    x_in = [sem(f"x_in{i}") for i in range(3)]
    raw_in = [sem(f"raw_in{i}") for i in range(2)]
    raw_split = [sem(f"raw_split{i}") for i in range(2)]
    res_in = [sem(f"res_in{i}") for i in range(4)]
    fg_in = sem("fg_in")
    out_done = [sem(f"out_done{i}") for i in range(2)]
    zeroed = sem("zeroed")
    dve_own = sem("dve_own")
    pool_own = sem("pool_own")
    lru_exp = sem("lru_exp")
    sp_in = sem("sp_in")
    sp_ready = sem("sp_ready")
    ssqx_ready = sem("ssqx_ready")
    rstdx_ready = sem("rstdx_ready")
    h_ready = sem("h_ready")
    xT_ready = sem("xT_ready")
    hhi_ready = sem("hhi_ready")
    hlo_ready = sem("hlo_ready")
    latw_hi = sem("latw_hi")
    z_ready = sem("z_ready")
    zstat_ready = sem("zstat_ready")
    rstdz_ready = sem("rstdz_ready")
    latn_ready = sem("latn_ready")
    latT_ready = sem("latT_ready")
    lathi_ready = sem("lathi_ready")
    kpe_half = sem("kpe_half")
    latlo_ready = sem("latlo_ready")
    cw_hi = sem("cw_hi")
    gw_hi = sem("gw_hi")
    gw_ready = sem("gw_ready")
    xr_hi_done = sem("xr_hi_done")
    xpad_ready = sem("xpad_ready")
    conv_done = sem("conv_done")
    xrs_ready = sem("xrs_ready")
    gate_ready = sem("gate_ready")
    sig_ready = sem("sig_ready")
    exp_ready = sem("exp_ready")
    min_ready = sem("min_ready")
    sqrt_ready = sem("sqrt_ready")
    scan_done = sem("scan_done")
    hsq_ready = sem("hsq_ready")
    hsq_summed = sem("hsq_summed")
    sg_ready = sem("sg_ready")
    gate_done = sem("gate_done")
    yr_done = sem("yr_done")
    ssr_ready = sem("ssr_ready")
    ssr_copied = sem("ssr_copied")
    aw_hi = sem("aw_hi")
    krope_hi = sem("krope_hi")
    krope_ready = sem("krope_ready")
    krope_copied = sem("krope_copied")
    misc_ready = sem("misc_ready")
    mhi_ready = sem("mhi_ready")
    misc_done = sem("misc_done")
    qrot_ready = sem("qrot_ready")
    qrope_hi = sem("qrope_hi")
    q_ready = sem("q_ready")
    s_ready = sem("s_ready")
    max_ready = sem("max_ready")
    p_ready = sem("p_ready")
    pt_ready = sem("pt_ready")
    pthi_ready = sem("pthi_ready")
    ptlo_ready = sem("ptlo_ready")
    pv_done = sem("pv_done")
    yT_copied = sem("yT_copied")
    wr_hi = sem("wr_hi")
    yr_hi_done = sem("yr_hi_done")
    yr_lo = sem("yr_lo")
    wm_hi = sem("wm_hi")
    ssm_ready = sem("ssm_ready")
    rstdm_ready = sem("rstdm_ready")
    rstdr_ready = sem("rstdr_ready")
    ymT_ready = sem("ymT_ready")
    ymf_ready = sem("ymf_ready")
    ymhi_ready = sem("ymhi_ready")
    ymlo_ready = sem("ymlo_ready")
    r_ready = sem("r_ready")
    r_added = sem("r_added")
    m_ready = sem("m_ready")
    m_added = sem("m_added")
    sso_ready = sem("sso_ready")
    rstdo_ready = sem("rstdo_ready")
    o_ready = sem("o_ready")

    w_in = a["w_in"][0].rearrange("(k p) n -> p k n", p=P)
    w_out = a["w_out"][0].rearrange("(k p) n -> p k n", p=P)
    w_q = a["w_q_b"][0].rearrange("(k p) (h e) -> p k h e", p=P, h=H)
    w_kv = a["w_kv_b"][0].rearrange("p (h two d) -> p two h d", two=2, d=VD)
    x_t = a["x"][0].rearrange("(t p) d -> t p d", p=P)
    out_t = out[0].rearrange("(t p) d -> t p d", p=P)

    USE_LAT, USE_CHUNK = 0, 4
    USE_Q, USE_KV = USE_CHUNK + len(CHUNKS), USE_CHUNK + len(CHUNKS) + 2
    USE_WR, USE_WM = USE_KV + 1, USE_KV + 1 + NC
    raw_parts = {}
    raw_parts[USE_Q] = raw_parts[USE_Q + 1] = 3
    raw_parts[USE_KV] = 2

    def raw_landed(use):
        return raw_in[use % 2], 16 * sum(raw_parts.get(u, 1) for u in range(use % 2, use + 1, 2))

    def split_of(use):
        return raw_split[use % 2], use // 2 + 1

    def passes(hi_a, lo_a, hi_b, lo_b):
        return ((hi_a, hi_b), (hi_a, lo_b), (lo_a, hi_b))

    def z_bank(m):
        return ps[:, 4 + m % 4, :]

    def z_use(c, half):
        return NT + 2 * c + half

    steps = attention_steps()
    MISC = [s for s in steps if s[0] in "VKQC"]
    FIRST_MISC = 8
    misc_no = {s: i for i, s in enumerate(MISC)}
    s_no = {s: i for i, s in enumerate(s for s in steps if s[0] == "S")}
    t_no = {("T",) + s[1:]: i for i, s in enumerate(s for s in steps if s[0] == "T")}
    q_no = {s: i for i, s in enumerate(s for s in steps if s[0] == "Q")}

    def misc_bank(i):
        return 4 + i % 4 if i < FIRST_MISC else 7

    def misc_before(i):
        if i < 4:
            return 0
        return i - 3 if i < FIRST_MISC else i

    SCORE_BANK = (0, 1, 2, 3, 0, 2, 0, 2)

    def scores_before(h, t):
        return max(0, NT * h + (-1, -1, 0, 0, 2, 4, 5, 6)[t])

    def tile_scores(t):
        b = SCORE_BANK[t]
        return ps[:, b:b + 2, :].rearrange("p b n -> p (b n)")[:, 0:P * (t + 1)] if t >= 4 else ps[:, b, 0:P * (t + 1)]

    def tile_probs(h, t):
        return probs[t, h % 2 if t in (4, 5) else 0]

    def query_tiles(n, j):
        return max(0, j - 4 * (n % 2))

    uses = [("R", 0)] + [u for t in range(NT) for u in ([("R", t + 1)] if t + 1 < NT else []) + [("M", t)]]

    def out_banks(kind, t):
        b = 2 * (uses.index((kind, t)) % 3)
        return ps[:, b:b + 2, :].rearrange("p b n -> p (b n)")

    block = ctx.enter_context(nc.Block())

    @block.sync
    def _(sp_):
        def load(t, src, s):
            sp_.dma_start(t, src).then_inc(s, 16)

        def x_load(t):
            if t >= 3:
                sp_.wait_ge(xT_ready, 2 * (t - 3) + 2)
            load(xst[t % 3][:, :], x_t[t], x_in[t % 3])

        def raw_load(use):
            dst = raw[use % 2]
            if use >= 2:
                sp_.wait_ge(*split_of(use - 2))
            s = raw_in[use % 2]
            if use < USE_CHUNK:
                load(dst[:, 0:2 * LAT].rearrange("p (k n) -> p k n", k=2), w_in[:, 2 * use:2 * use + 2, 0:LAT], s)
            elif use < USE_Q:
                col = CHUNKS[use - USE_CHUNK][2]
                load(dst[:, :].rearrange("p (k n) -> p k n", k=KD), w_in[:, :, col:col + P], s)
            elif use < USE_KV:
                k = use - USE_Q
                d = dst[:, :].rearrange("p (h n) -> p h n", h=H)
                load(d[:, :, 0:QK], w_q[:, k, :, :], s)
                load(d[:, :, QK:QK + 16], w_q[:, k, :, NOPE + 16:QK], s)
                load(d[:, :, QK + 16:P], w_q[:, k, :, NOPE:NOPE + 16], s)
            elif use == USE_KV:
                d = dst[:, :].rearrange("p (two h d) -> p two h d", two=2, h=H)
                load(d[:, 0, :, :], w_kv[:, 0, :, :], s)
                load(d[:, 1, :, :], w_kv[:, 1, :, :], s)
            elif use < USE_WM:
                load(dst[:, :], w_out[:, NC + use - USE_WR, :], s)
            else:
                load(dst[:, :], w_out[:, use - USE_WM, :], s)

        x_load(0)
        load(ident[:, :], a["ident"], first_in)
        load(g_in_row[:, :], a["norm_in_g"].to_broadcast((P, D)), first_in)
        raw_load(0)
        raw_load(1)
        x_load(1)
        load(g_lat_row[:, 0:QR], a["q_norm_g"].to_broadcast((P, QR)), const_in)
        load(g_lat_row[:, QR:], a["kv_norm_g"].to_broadcast((P, KVR)), const_in)
        raw_load(2)
        raw_load(3)
        x_load(2)
        load(trig[NOPE:P, :], a["trig"], const_in)
        load(stack[:, :], a["stack"], const_in)
        with nc.allow_non_contiguous_dma(reason="a few per-channel parameters"):
            for t, name in ((g_mla, "out_norm_mla_g"), (g_rnn, "out_norm_rnn_g"), (conv_b, "conv_b"),
                            (bias_a, "b_rg_a"), (bias_x, "b_rg_x"), (lru, "lru_param")):
                load(t[:, :], a[name][0].rearrange("(c p) -> p c", p=P), const_in)
            load(conv_w[:, :, :], a["conv_w"][0].rearrange("k (c p) -> p k c", p=P), const_in)
        sp_.wait_ge(zeroed, 1)
        for g, name in enumerate(("w_rg_a", "w_rg_x")):
            w = a[name][0].rearrange("(c two) i j -> two i c j", two=2)
            for b in range(2):
                load(gate_raw[64 * b:64 * b + 64, g, :, 64 * b:64 * b + 64], w[b], gates_in)
        x_load(3)
        raw_load(4)
        x_load(4)
        raw_load(5)
        for t in range(5, NT):
            x_load(t)
        for use in range(6, USE_WR + 2):
            raw_load(use)
        for use in range(USE_WR + 2, USE_WM + NC):
            raw_load(use)
        sp_.wait_ge(pv_done, len(t_no))
        load(fg_row[:, :], a["final_norm_g"].rearrange("(o d) -> o d", o=1).to_broadcast((P, D)), fg_in)
        for t in range(4):
            load(xres[t][:, :], x_t[t], res_in[t])
        for t in range(NT):
            sp_.wait_ge(o_ready, t + 1)
            load(out_t[t], ost[t % 2][:, :], out_done[t % 2])
            if t + 4 < NT:
                load(xres[t % 4][:, :], x_t[t + 4], res_in[t % 4])
        for i in range(2):
            sp_.wait_ge(out_done[i], 16 * NT // 2)

    N_CONST = 2 + 2 + 6 + 1

    @block.tensor
    def _(pe):
        def transpose_h(t):
            pe.wait_ge(h_ready, t + 1)
            for b in range(2):
                if t >= 1:
                    pe.wait_ge(hlo_ready, 2 * (t - 1) + b + 1)
                for k in range(4):
                    mm = pe.transpose(ps[:, b, P * k:P * k + P], xst[t % 3][:, P * (4 * b + k):P * (4 * b + k) + P], ident[:, :])
                mm.then_inc(xT_ready, 1)

        def z_free(m):
            if m < 4:
                return
            u = m - 4
            if u < NT:
                pe.wait_ge(latn_ready, u + 1)
            else:
                kind, c, _ = CHUNKS[(u - NT) // 2]
                if kind == "x":
                    pe.wait_ge(xpad_ready, u - NT + 1)
                else:
                    pe.wait_ge(gate_done, u - NT - 2 * NC + 1)

        def latents(t):
            z_free(t)
            for b in range(2):
                pe.wait_ge(hlo_ready, 2 * t + b + 1)
                for k in range(4 * b, 4 * b + 4):
                    if t == 0 and k % 2 == 0:
                        pe.wait_ge(*split_of(USE_LAT + k // 2))
                    for n, (l, r) in enumerate(passes(hT_h, hT_l, lat_w_h, lat_w_l)):
                        mm = pe.matmul(z_bank(t)[:, 0:LAT], l[:, k, P * t:P * t + P], r[:, k, :],
                                       start=(k == 0 and n == 0), stop=(k == KD - 1 and n == 2))
            mm.then_inc(z_ready, 1)

        def transpose_latents(t):
            pe.wait_ge(latn_ready, t + 1)
            pe.wait_ge(zstat_ready, t + 1)
            if t >= 1:
                pe.wait_ge(latlo_ready, t)
            for k in range(3):
                pe.transpose(ps[:, 2, P * k:P * k + P], latn[t % 2][:, P * k:P * k + P], ident[:, :])
            pe.transpose(ps[:, 2, 3 * P:4 * P], krs[t % 2][:, :], ident[:, :]).then_inc(latT_ready, 1)

        def chunk(c, half):
            if half == 0:
                pe.wait_ge(*split_of(USE_CHUNK + c))
            m = z_use(c, half)
            z_free(m)
            for k in range(KD):
                for n, (l, r) in enumerate(passes(cw_h[c % 2], cw_l[c % 2], hT_h, hT_l)):
                    mm = pe.matmul(z_bank(m), l[:, k, :], r[:, k, HALF * half:HALF * half + HALF],
                                   start=(k == 0 and n == 0), stop=(k == KD - 1 and n == 2))
            mm.then_inc(z_ready, 1)

        def gates(c):
            if c == 0:
                pe.wait_ge(gw_ready, 1)
            pe.wait_ge(xrs_ready, c + 1)
            for g in range(2):
                for half in range(2):
                    u = 4 * c + 2 * g + half
                    if u >= 4:
                        pe.wait_ge(sig_ready, u - 3)
                    elif u == 0:
                        pe.wait_ge(latlo_ready, NT)
                    for n, (l, r) in enumerate(passes(gw_h, gw_l, xr_h, xr_l)):
                        mm = pe.matmul(ps[:, u % 4, :], l[:, g, c, :], r[:, HALF * half:HALF * half + HALF],
                                       start=(n == 0), stop=(n == 2))
                    mm.then_inc(gate_ready, 1)

        pe.wait_ge(first_in, 32)
        transpose_h(0)
        for t in range(NT):
            if t + 1 < NT:
                transpose_h(t + 1)
            latents(t)
            if t >= 1:
                transpose_latents(t - 1)
        for c in range(len(CHUNKS)):
            chunk(c, 0)
            if c == 0:
                transpose_latents(NT - 1)
            chunk(c, 1)
            if 2 <= c < 2 + NC:
                gates(c - 2)

        pe.wait_ge(hsq_summed, NC - 1)
        pe.wait_ge(sig_ready, 4 * NC)
        for t in range(NT):
            mm = pe.matmul(ps[:, 0, t:t + 1], sq_sum[:, P * t:P * t + P], one_col[:, :], start=True, stop=True)
        mm.then_inc(ssr_ready, 1)

        def misc(step):
            i = misc_no[step]
            if misc_before(i):
                pe.wait_ge(misc_done, misc_before(i))
            if i < 4:
                pe.wait_ge(gate_done, 4 * NC)
            bank = ps[:, misc_bank(i), :]
            kind = step[0]
            if i == 0:
                for use in range(USE_Q, USE_KV + 1):
                    pe.wait_ge(*split_of(use))
            if kind == "V":
                _, half, part = step
                for jj in range(2):
                    j = 2 * part + jj
                    for n, (l, r) in enumerate(passes(latT_h, latT_l, wkv_h, wkv_l)):
                        mm = pe.matmul(bank[:, 256 * jj:256 * jj + 256], l[:, 2, P * j:P * j + P],
                                       r[:, 512 + 256 * half:768 + 256 * half], start=(n == 0 and jj == 0), stop=(n == 2),
                                       skip_group_check=True)
            elif kind == "K":
                _, pair, half = step
                for n, (l, r) in enumerate(passes(wkv_h, wkv_l, latT_h, latT_l)):
                    mm = pe.matmul(bank, l[:, P * pair:P * pair + P], r[:, 2, HALF * half:HALF * half + HALF],
                                   start=(n == 0), stop=(n == 2))
            elif kind == "Q":
                _, h, half = step
                for k in range(2):
                    for n, (l, r) in enumerate(passes(wq_h, wq_l, latT_h, latT_l)):
                        mm = pe.matmul(bank, l[:, k, h, :], r[:, k, HALF * half:HALF * half + HALF],
                                       start=(k == 0 and n == 0), stop=(k == 1 and n == 2))
            else:
                _, n_item = step
                pe.wait_ge(yT_copied, n_item + 1)
                for tt in range(4):
                    mm = pe.matmul(bank[:, VD * tt:VD * tt + VD], yTs[:, P * tt:P * tt + P], stack[:, :],
                                   start=(tt == 0), stop=True, skip_group_check=True)
            mm.then_inc(misc_ready, 1)

        def scores(h, t):
            k = s_no[("S", h, t)]
            pe.wait_ge(q_ready, 2 * h + 1 + t // 4)
            pe.wait_ge(misc_done, misc_no[("K", h // 2, t // 4)] + 1)
            if h == 0:
                pe.wait_ge(krope_ready, 1)
            elif h < 4:
                pe.wait_ge(krope_copied, 2 * h)
            if scores_before(h, t):
                pe.wait_ge(p_ready, scores_before(h, t))
            elif t == 0:
                pe.wait_ge(ssr_copied, 1)
            n_keys = P * (t + 1)
            chunks = [(0, min(HALF, n_keys))] + ([(HALF, n_keys)] if n_keys > HALF else [])
            q0 = P * t
            b0 = SCORE_BANK[t]
            kslot = 2 * (h // 2 % 2) + h % 2
            for n, (q, ks) in enumerate(((qh, (kh, kl)), (ql, (kh,)))):
                for m, kk in enumerate(ks):
                    for c, (lo, hi) in enumerate(chunks):
                        mm = pe.matmul(ps[:, b0 + c, 0:hi - lo], q[0:QK, q0:q0 + P], kk[0:QK, kslot, lo:hi],
                                       start=(n == 0 and m == 0), stop=(n == 1), skip_group_check=True)
                if n == 0:
                    c = len(chunks) - 1
                    pe.matmul(ps[:, b0 + c, n_keys - 64 - chunks[c][0]:n_keys - chunks[c][0]], half_rows[:, :],
                              masked[:, :], start=False, stop=False, skip_group_check=True)
            mm.then_inc(s_ready, 1)

        def transpose_probs(n, j):
            h, g = divmod(n, 2)
            u = t_no[("T", n, j)]
            if j == 0:
                pe.wait_ge(p_ready, NT * h + 4 * g + 4)
            if u >= 2:
                pe.wait_ge(ptlo_ready, u - 1)
            elif u == 0:
                pe.wait_ge(misc_done, FIRST_MISC)
            for tt in range(query_tiles(n, j), 4):
                mm = pe.transpose(ps[:, 4 + u % 2, P * tt:P * tt + P], tile_probs(h, 4 * g + tt)[:, P * j:P * j + P], ident[:, :])
            mm.then_inc(pt_ready, 1)

        def pv(n, j):
            h, g = divmod(n, 2)
            u = t_no[("T", n, j)]
            pe.wait_ge(ptlo_ready, u + 1)
            if j == 0:
                pe.wait_ge(misc_done, misc_no[("V", h // 4, 1 if g == 0 else 3)] + 1)
                if n >= 1:
                    pe.wait_ge(yT_copied, n)
            c0 = P * query_tiles(n, j)
            for m, pt in enumerate((pth, ptl)):
                mm = pe.matmul(ps[:, 6, c0:HALF], vv[:, j, h % 4, :], pt[u % 2][:, c0:HALF],
                               start=(j == 0 and m == 0), stop=(j == 4 * g + 3 and m == 1), skip_group_check=True)
            mm.then_inc(pv_done, 1)

        for step in steps:
            if step[0] in "VKQC":
                misc(step)
            elif step[0] == "S":
                scores(*step[1:])
            elif step[0] == "T":
                transpose_probs(*step[1:])
            elif step[0] == "PV":
                pv(*step[1:])

        def transpose_y(t):
            pe.wait_ge(misc_done, len(MISC))
            if t >= 2:
                pe.wait_ge(ymf_ready, t - 1)
            for b in range(NC):
                mm = pe.transpose(ps[:, 6 + t % 2, P * b:P * b + P], ynat[:, t, P * b:P * b + P], ident[:, :])
            mm.then_inc(ymT_ready, 1)

        def project(kind, t, ys_h, ys_l, w_h, w_l):
            i = uses.index((kind, t))
            if i >= 3:
                k, tb = uses[i - 3]
                pe.wait_ge(r_added if k == "R" else m_added, tb + 1)
            elif i == 0:
                pe.wait_ge(p_ready, H * NT)
                pe.wait_ge(ptlo_ready, len(t_no))
            b0 = 2 * (i % 3)
            for c in range(NC):
                if kind == "R" and t == 0:
                    pe.wait_ge(*split_of(USE_WR + c))
                    pe.wait_ge(yr_lo, c + 1)
                if kind == "M" and t == 0:
                    pe.wait_ge(*split_of(USE_WM + c))
                for n, (l, r) in enumerate(passes(ys_h, ys_l, w_h, w_l)):
                    for half in range(2):
                        mm = pe.matmul(ps[:, b0 + half, :], l(c), r[c][:, HALF * half:HALF * half + HALF],
                                       start=(c == 0 and n == 0), stop=(c == NC - 1 and n == 2), skip_group_check=True)
            mm.then_inc(r_ready if kind == "R" else m_ready, 1)

        def project_r(t):
            project("R", t, lambda c: yr_h[c][:, P * t:P * t + P], lambda c: yr_l[c][:, P * t:P * t + P], wr_h, wr_l)

        def project_m(t):
            pe.wait_ge(ymlo_ready, t + 1)
            project("M", t, lambda c: ym_h[t % 2][:, c, :], lambda c: ym_l[t % 2][:, c, :], wm_h, wm_l)

        transpose_y(0)
        project_r(0)
        for t in range(NT):
            if t + 1 < NT:
                transpose_y(t + 1)
                project_r(t + 1)
            project_m(t)

    @block.scalar
    def _(act):
        def split_latent_weights(k):
            s, v = raw_landed(USE_LAT + k)
            act.wait_ge(s, v)
            act.activation(lat_w_h[:, 2 * k:2 * k + 2, :], raw[k % 2][:, 0:2 * LAT].rearrange("p (k n) -> p k n", k=2),
                           ACT.Copy).then_inc(latw_hi, 1)

        def square_x(t):
            act.wait_ge(x_in[t % 3], 16 * (t // 3 + 1))
            if t >= 3:
                act.wait_ge(ssqx_ready, t - 2)
            act.activation(junk[t % 3], xst[t % 3][:, :], ACT.Square, accum_out=ssq_x[:, t:t + 1]).then_inc(ssqx_ready, 1)

        def h_hi(t):
            for b in range(2):
                act.wait_ge(xT_ready, 2 * t + b + 1)
                act.activation(hT_h[:, 4 * b:4 * b + 4, P * t:P * t + P],
                               ps[:, b, :].rearrange("p (k n) -> p k n", k=4), ACT.Copy).then_inc(hhi_ready, 1)

        def latent_stats(t):
            act.wait_ge(z_ready, t + 1)
            z = z_bank(t)
            unused = yrT[:, :, :].rearrange("p c n -> p (c n)")[:, (QR + KVR) * t:(QR + KVR) * (t + 1)]
            act.activation(unused[:, 0:QR], z[:, 0:QR], ACT.Square, accum_out=ssq_z[:, t, 0:1])
            act.activation(unused[:, QR:], z[:, QR:QR + KVR], ACT.Square, accum_out=ssq_z[:, t, 1:2])
            if t >= 2:
                act.wait_ge(latT_ready, t - 1)
            kr = krs[t % 2]
            act.activation(kr[:, 64:96], z[:, QR + KVR:LAT], ACT.Copy)
            act.activation(kr[:, 96:112], z[:, QR + KVR + 16:LAT], ACT.Copy)
            act.activation(kr[:, 112:128], z[:, QR + KVR:QR + KVR + 16], ACT.Copy).then_inc(zstat_ready, 1)

        def latents_hi(t):
            act.wait_ge(latT_ready, t + 1)
            act.activation(latT_h[:, :, P * t:P * t + P], ps[:, 2, 0:3 * P].rearrange("p (k n) -> p k n", k=3),
                           ACT.Copy).then_inc(lathi_ready, 1)

        square_x(0)
        split_latent_weights(0)
        split_latent_weights(1)
        h_hi(0)
        square_x(1)
        split_latent_weights(2)
        split_latent_weights(3)
        act.wait_ge(sp_in, 1)
        act.activation(sp[:, 2, :], sp[:, 1, :], ACT.Exp, scale=-1.0).then_inc(lru_exp, 1)
        for i in range(1, NT + 3):
            if 2 <= i < NT:
                square_x(i)
            if 2 <= i <= NT:
                h_hi(i - 1)
            if 2 <= i <= NT + 1:
                latent_stats(i - 2)
            if 3 <= i:
                latents_hi(i - 3)

        def gate_sigmoid(c, g):
            dst, bias = ((ra, bias_a), (iu, bias_x))[g]
            for half in range(2):
                u = 4 * c + 2 * g + half
                act.wait_ge(gate_ready, u + 1)
                if c >= 1 and half == 0:
                    act.wait_ge(scan_done, c)
                act.activation(dst[:, HALF * half:HALF * half + HALF], ps[:, u % 4, :], ACT.Sigmoid,
                               bias=bias[:, c:c + 1]).then_inc(sig_ready, 1)

        def decay(c):
            act.wait_ge(sig_ready, 4 * c + 4)
            if c == 0:
                act.wait_ge(sp_ready, 1)
            if c >= 1:
                act.wait_ge(yr_done, c)
            act.activation(mh[:, :], ra[:, :], ACT.Exp, scale=sp16[:, c:c + 1]).then_inc(exp_ready, 1)
            act.activation(ra[:, :], ra[:, :], ACT.Exp, scale=sp8[:, c:c + 1]).then_inc(exp_ready, 1)
            act.wait_ge(min_ready, c + 1)
            act.activation(mh[:, :], mh[:, :], ACT.Sqrt, bias=1.0).then_inc(sqrt_ready, 1)

        def square_h(c):
            act.wait_ge(scan_done, c + 1)
            if c >= 2:
                act.wait_ge(hsq_summed, c - 1)
            act.activation(sq_sum[:, :] if c == 0 else hsq[:, :], mh[:, :], ACT.Square).then_inc(hsq_ready, 1)

        def chunk_out(c):
            kind, cc, _ = CHUNKS[c]
            for half in range(2):
                m = z_use(c, half)
                act.wait_ge(z_ready, m + 1)
                if kind == "x":
                    if cc >= 1 and half == 0:
                        act.wait_ge(conv_done, cc)
                    if cc == 0 and half == 0:
                        act.wait_ge(latlo_ready, NT)
                    act.activation(xpad[:, 3 + HALF * half:3 + HALF * half + HALF], z_bank(m), ACT.Copy).then_inc(xpad_ready, 1)
                else:
                    u = 2 * (c - NC) + half
                    if u >= 2:
                        act.wait_ge(gate_done, u - 1)
                    act.activation(sg[u % 2][:, :], z_bank(m), ACT.Sigmoid).then_inc(sg_ready, 1)

        for c in range(len(CHUNKS)):
            if 3 <= c < 3 + NC:
                gate_sigmoid(c - 3, 0)
                gate_sigmoid(c - 3, 1)
            chunk_out(c)
            if 4 <= c < 4 + NC:
                square_h(c - 4)
            if 3 <= c < 3 + NC:
                decay(c - 3)

        act.wait_ge(z_ready, NT + 2 * len(CHUNKS))
        act.activation(kh[64:96, 0, :], kpe[64:96, :], ACT.Copy).then_inc(krope_hi, 1)

        def misc_hi(step):
            i = misc_no[step]
            kind = step[0]
            bank = ps[:, misc_bank(i), :]
            if kind == "C":
                return
            act.wait_ge(misc_ready, i + 1)
            if kind == "V":
                _, half, part = step
                if half == 1:
                    act.wait_ge(pv_done, t_no[("T", 7, 2 * part + 1)] + 1)
                act.activation(vv[:, 2 * part:2 * part + 2, :, 0:VD],
                               bank.rearrange("p (j h d) -> p j h d", j=2, h=4), ACT.Copy).then_inc(mhi_ready, 1)
            elif kind == "K":
                _, pair, half = step
                if pair >= 2:
                    act.wait_ge(s_ready, s_no[("S", 2 * pair - 3, 7)] + 1)
                c = slice(HALF * half, HALF * half + HALF)
                act.activation(kh[0:64, 2 * (pair % 2), c], bank[0:64, :], ACT.Copy)
                act.activation(kh[0:64, 2 * (pair % 2) + 1, c], bank[64:128, :], ACT.Copy).then_inc(mhi_ready, 1)
            else:
                _, h, half = step
                if h >= 1:
                    act.wait_ge(s_ready, s_no[("S", h - 1, 4 * half + 3)] + 1)
                c = slice(HALF * half, HALF * half + HALF)
                act.activation(qh[0:64, c], bank[0:64, :], ACT.Copy).then_inc(mhi_ready, 1)

        def exponentials(h, t):
            k = s_no[("S", h, t)]
            act.wait_ge(max_ready, k + 1)
            before = h - (2 if t in (4, 5) else 1)
            if before >= 0:
                act.wait_ge(pt_ready, t_no[("T", 2 * before + t // 4, t)] + 1)
            act.activation(tile_probs(h, t)[:, :], tile_scores(t), ACT.Exp, bias=bias_s[:, NT * h + t:NT * h + t + 1], scale=SCALE,
                           accum_out=rsum[:, NT * h + t:NT * h + t + 1]).then_inc(p_ready, 1)

        def probs_hi(n, j):
            u = t_no[("T", n, j)]
            act.wait_ge(pt_ready, u + 1)
            if u >= 2:
                act.wait_ge(pv_done, u - 1)
            c0 = P * query_tiles(n, j)
            act.activation(pth[u % 2][:, c0:HALF], ps[:, 4 + u % 2, c0:HALF], ACT.Copy).then_inc(pthi_ready, 1)

        def copy_y(n):
            act.wait_ge(pv_done, t_no[("T", n, 4 * (n % 2) + 3)] + 1)
            if n >= 1:
                act.wait_ge(misc_ready, misc_no[("C", n - 1)] + 1)
            act.activation(yTs[:, :], ps[:, 6, :], ACT.Copy).then_inc(yT_copied, 1)

        for step in scores_after_transposes(steps):
            if step[0] in "VKQC":
                misc_hi(step)
            elif step[0] == "S":
                exponentials(*step[1:])
            elif step[0] == "T":
                probs_hi(*step[1:])
            elif step[0] == "Y":
                copy_y(*step[1:])

        def split_wm(c):
            s, v = raw_landed(USE_WM + c)
            act.wait_ge(s, v)
            act.activation(wm_h[c][:, :], raw[(USE_WM + c) % 2][:, :], ACT.Copy).then_inc(wm_hi, 1)

        def square_y(t):
            act.wait_ge(misc_done, len(MISC))
            if t >= 2:
                act.wait_ge(ssm_ready, t - 1)
            act.activation(trig[:, HALF * (t % 2):HALF * (t % 2) + HALF], ynat[:, t, :], ACT.Square, accum_out=ssq_m[:, t:t + 1]).then_inc(ssm_ready, 1)

        def y_hi(t):
            act.wait_ge(ymf_ready, t + 1)
            if t >= 2:
                act.wait_ge(m_ready, t - 1)
            act.activation(ym_h[t % 2][:, :, :], ymf[:, :, :], ACT.Copy).then_inc(ymhi_ready, 1)

        act.wait_ge(pt_ready, len(t_no))
        act.wait_ge(pv_done, len(t_no))
        for c in range(NC):
            split_wm(c)
            if c == 0:
                y_hi(0)
            square_y(c)

        def square_out(t):
            act.wait_ge(m_added, t + 1)
            if t >= 4:
                act.wait_ge(sso_ready, t - 3)
            act.activation(yrT[:, t % 4, :], xres[t % 4][:, :], ACT.Square, accum_out=ssq_o[:, t:t + 1]).then_inc(sso_ready, 1)

        act.wait_ge(yr_lo, NC)
        for t in range(1, NT):
            y_hi(t)
            if t + 3 < NT:
                square_y(t + 3)
            if t >= 2:
                square_out(t - 2)
        square_out(NT - 2)
        square_out(NT - 1)

    @block.vector
    def _(dve):
        own = [0]

        def after(ins):
            own[0] += 1
            ins.then_inc(dve_own, 1)
            dve.wait_ge(dve_own, own[0])

        def split_latent_weights(k):
            dve.wait_ge(latw_hi, k + 1)
            r = raw[k % 2][:, 0:2 * LAT].rearrange("p (k n) -> p k n", k=2)
            dve.tensor_tensor(lat_w_l[:, 2 * k:2 * k + 2, :], r, f32(lat_w_h[:, 2 * k:2 * k + 2, :]), ALU.subtract)\
               .then_inc(raw_split[k % 2], 1)

        def normalise_x(t):
            dve.wait_ge(rstdx_ready, t + 1)
            x = xst[t % 3]
            dve.scalar_tensor_tensor(x[:, :], x[:, :], rstd_x[:, t:t + 1], g_in_row[:, :], ALU.mult, ALU.mult)\
               .then_inc(h_ready, 1)

        def h_lo(t):
            for b in range(2):
                dve.wait_ge(hhi_ready, 2 * t + b + 1)
                dve.tensor_tensor(hT_l[:, 4 * b:4 * b + 4, P * t:P * t + P], ps[:, b, :].rearrange("p (k n) -> p k n", k=4),
                                  f32(hT_h[:, 4 * b:4 * b + 4, P * t:P * t + P]), ALU.subtract).then_inc(hlo_ready, 1)

        def normalise_latents(t):
            dve.wait_ge(rstdz_ready, t + 1)
            if t >= 2:
                dve.wait_ge(latT_ready, t - 1)
            z = z_bank(t)
            dve.scalar_tensor_tensor(latn[t % 2][:, 0:QR], z[:, 0:QR], rstd_z[:, t, 0:1], g_lat_row[:, 0:QR], ALU.mult, ALU.mult)
            dve.scalar_tensor_tensor(latn[t % 2][:, QR:], z[:, QR:QR + KVR], rstd_z[:, t, 1:2], g_lat_row[:, QR:],
                                     ALU.mult, ALU.mult).then_inc(latn_ready, 1)

        def latents_lo(t):
            c = slice(P * t, P * t + P)
            dve.wait_ge(lathi_ready, t + 1)
            dve.tensor_tensor(latT_l[:, :, c], ps[:, 2, 0:3 * P].rearrange("p (k n) -> p k n", k=3),
                              f32(latT_h[:, :, c]), ALU.subtract)
            kr = ps[:, 2, 3 * P:4 * P]
            dve.tensor_tensor(rope_t[64:96, :], kr[96:128, :], trig[96:128, c], ALU.mult)
            dve.tensor_tensor(kpe[64:96, c], kr[64:96, :], trig[64:96, c], ALU.mult).then_inc(kpe_half, 1)
            dve.wait_ge(kpe_half, t + 1)
            dve.tensor_tensor(kpe[64:96, c], kpe[64:96, c], rope_t[64:96, :], ALU.add).then_inc(latlo_ready, 1)

        def softplus_start():
            after(dve.tensor_scalar(sp[:, 0, :], lru[:, :], -1.0, None, ALU.mult))
            dve.tensor_tensor(sp[:, 1, :], lru[:, :], sp[:, 0, :], ALU.max).then_inc(sp_in, 1)

        def softplus_end():
            e, w, w2, s = sp[:, 2, :], sp[:, 3, :], sp[:, 4, :], sp[:, 5, :]
            dve.wait_ge(lru_exp, 1)
            after(dve.tensor_scalar(sp[:, 6, :], e, 2.0, None, ALU.add))
            after(dve.reciprocal(sp[:, 7, :], sp[:, 6, :]))
            after(dve.tensor_tensor(w, e, sp[:, 7, :], ALU.mult))
            after(dve.tensor_tensor(w2, w, w, ALU.mult))
            after(dve.tensor_scalar(s, w2, 1.0 / 17.0, None, ALU.mult))
            for n in (15.0, 13.0, 11.0, 9.0, 7.0, 5.0, 3.0):
                after(dve.scalar_tensor_tensor(s, s, 1.0 / n, w2, ALU.add, ALU.mult))
            after(dve.scalar_tensor_tensor(s, s, 1.0, w, ALU.add, ALU.mult))
            after(dve.tensor_scalar(sp[:, 8, :], sp[:, 0, :], 0.0, None, ALU.max))
            after(dve.scalar_tensor_tensor(sp[:, 9, :], s, 2.0, sp[:, 8, :], ALU.mult, ALU.add))
            after(dve.tensor_scalar(sp8[:, :], sp[:, 9, :], -8.0, None, ALU.mult))
            dve.tensor_scalar(sp16[:, :], sp[:, 9, :], -16.0, None, ALU.mult).then_inc(sp_ready, 1)

        dve.memset(one_col[:, :], 1.0)
        dve.memset(half_rows[:, :], 0.0)
        after(dve.memset(masked[:, :], MASKED))
        dve.memset(half_rows[:, 0:64], 1.0)
        dve.memset(krs[0][:, :], 0.0)
        after(dve.memset(krs[1][:, :], 0.0))
        dve.wait_ge(first_in, 32)
        normalise_x(0)
        split_latent_weights(0)
        split_latent_weights(1)
        h_lo(0)
        normalise_x(1)
        split_latent_weights(2)
        split_latent_weights(3)
        dve.wait_ge(const_in, 16 * N_CONST)
        softplus_start()
        for i in range(1, NT + 3):
            if 2 <= i < NT:
                normalise_x(i)
            if 2 <= i <= NT:
                h_lo(i - 1)
            if i == 3:
                softplus_end()
            if 2 <= i <= NT + 1:
                normalise_latents(i - 2)
            if 3 <= i:
                latents_lo(i - 3)

        def convolve(c):
            dve.wait_ge(xpad_ready, 2 * c + 2)
            if c == 1:
                dve.wait_ge(gw_ready, 1)
            y = xr[c]
            after(dve.tensor_scalar(y, xpad[:, 3:3 + SEQ], conv_w[:, 3, c:c + 1], conv_b[:, c:c + 1], ALU.mult, ALU.add))
            for k in range(2, 0, -1):
                after(dve.scalar_tensor_tensor(y, xpad[:, k:k + SEQ], conv_w[:, k, c:c + 1], y, ALU.mult, ALU.add))
            dve.scalar_tensor_tensor(y, xpad[:, 0:SEQ], conv_w[:, 0, c:c + 1], y, ALU.mult, ALU.add).then_inc(conv_done, 1)

        def gated_input(c):
            dve.wait_ge(sig_ready, 4 * c + 4)
            dve.wait_ge(conv_done, c + 1)
            dve.tensor_tensor(iu[:, :], iu[:, :], xr[c], ALU.mult)
            dve.wait_ge(exp_ready, 2 * c + 1)
            dve.tensor_scalar(mh[:, :], mh[:, :], 1.0, -1.0, ALU.min, ALU.mult).then_inc(min_ready, 1)

        def recur(c):
            dve.wait_ge(sqrt_ready, c + 1)
            after(dve.memset(mh[:, 0:1], 1.0))
            after(dve.scalar_tensor_tensor(iu[:, :], mh[:, :], 1e-6, iu[:, :], ALU.max, ALU.mult))
            dve.wait_ge(exp_ready, 2 * c + 2)
            dve.tensor_tensor_scan(mh[:, :], ra[:, :], iu[:, :], 0.0, ALU.mult, ALU.add).then_inc(scan_done, 1)

        def gate_out(c):
            kind, cc, _ = CHUNKS[c]
            dst, gain = (yrT, g_rnn) if kind == "gr" else (gmT, g_mla)
            for half in range(2):
                u = 2 * (c - NC) + half
                dve.wait_ge(sg_ready, u + 1)
                dve.scalar_tensor_tensor(dst[:, cc, HALF * half:HALF * half + HALF], z_bank(z_use(c, half)),
                                         gain[:, cc:cc + 1], sg[u % 2][:, :], ALU.mult, ALU.mult).then_inc(gate_done, 1)

        def gate_h(c):
            dve.wait_ge(scan_done, c + 1)
            dve.wait_ge(hsq_ready, c + 1)
            dve.wait_ge(gate_done, 2 * c + 2)
            dve.tensor_tensor(yrT[:, c, :], yrT[:, c, :], mh[:, :], ALU.mult).then_inc(yr_done, 1)

        for c in range(len(CHUNKS)):
            if c == 0:
                dve.wait_ge(z_ready, NT)
                after(dve.memset(xpad[:, 0:3], 0.0))
            if c < NC:
                convolve(c)
            else:
                gate_out(c)
            if 4 <= c < 4 + NC:
                gate_h(c - 4)
            if 3 <= c < 3 + NC:
                gated_input(c - 3)
                recur(c - 3)

        dve.wait_ge(ssr_ready, 1)
        dve.tensor_copy(ssq_r[:, :], ps[:, 0, 0:NT]).then_inc(ssr_copied, 1)
        dve.wait_ge(krope_hi, 1)
        dve.tensor_tensor(kl[64:96, 0, :], kpe[64:96, :], f32(kh[64:96, 0, :]), ALU.subtract).then_inc(krope_ready, 1)

        def misc_lo(step):
            i = misc_no[step]
            kind = step[0]
            bank = ps[:, misc_bank(i), :]
            if kind == "C":
                _, n = step
                h, g = divmod(n, 2)
                r = slice(NT * h + 4 * g, NT * h + 4 * g + 4)
                dve.wait_ge(p_ready, s_no[("S", h, 4 * g + 3)] + 1)
                after(dve.reciprocal(rinv[:, r], rsum[:, r]))
                dve.wait_ge(misc_ready, i + 1)
                dve.tensor_tensor(ynat[:, 4 * g:4 * g + 4, VD * h:VD * h + VD],
                                  bank[:, 0:4 * VD].rearrange("p (t d) -> p t d", t=4),
                                  rinv[:, r].rearrange("p (t o) -> p t o", o=1).to_broadcast((P, 4, VD)), ALU.mult)\
                   .then_inc(misc_done, 1)
                return
            dve.wait_ge(mhi_ready, i + 1 - sum(s[0] == "C" for s in MISC[:i]))
            if kind == "V":
                _, half, part = step
                j = slice(2 * part, 2 * part + 2)
                dve.tensor_tensor(vv[:, j, :, VD:P], bank.rearrange("p (j h d) -> p j h d", j=2, h=4),
                                  f32(vv[:, j, :, 0:VD]), ALU.subtract).then_inc(misc_done, 1)
            elif kind == "K":
                _, pair, half = step
                c = slice(HALF * half, HALF * half + HALF)
                b = 2 * (pair % 2)
                dve.tensor_tensor(kl[0:64, b, c], bank[0:64, :], f32(kh[0:64, b, c]), ALU.subtract)
                dve.tensor_tensor(kl[0:64, b + 1, c], bank[64:128, :], f32(kh[0:64, b + 1, c]), ALU.subtract).then_inc(misc_done, 1)
            else:
                _, h, half = step
                c = slice(HALF * half, HALF * half + HALF)
                u = 2 * h + half
                dve.tensor_tensor(ql[0:64, c], bank[0:64, :], f32(qh[0:64, c]), ALU.subtract)
                if u >= 1:
                    dve.wait_ge(q_ready, u)
                dve.tensor_tensor(qt[0][64:96, :], bank[96:128, :], trig[96:128, c], ALU.mult)
                dve.tensor_tensor(qt[1][64:96, :], bank[64:96, :], trig[64:96, c], ALU.mult).then_inc(misc_done, 1)
                dve.wait_ge(misc_done, i + 1)
                dve.tensor_tensor(qt[1][64:96, :], qt[1][64:96, :], qt[0][64:96, :], ALU.add).then_inc(qrot_ready, 1)

        def row_max(h, t):
            k = s_no[("S", h, t)]
            i = NT * h + t
            dve.wait_ge(s_ready, k + 1)
            after(dve.tensor_reduce(nmax[:, i:i + 1], tile_scores(t), AX.X, ALU.max))
            dve.tensor_scalar(bias_s[:, i:i + 1], nmax[:, i:i + 1], -SCALE, None, ALU.mult).then_inc(max_ready, 1)

        def probs_lo(n, j):
            u = t_no[("T", n, j)]
            dve.wait_ge(pthi_ready, u + 1)
            c0 = P * query_tiles(n, j)
            dve.tensor_tensor(ptl[u % 2][:, c0:HALF], ps[:, 4 + u % 2, c0:HALF], f32(pth[u % 2][:, c0:HALF]), ALU.subtract)\
               .then_inc(ptlo_ready, 1)

        for step in steps:
            if step[0] in "VKQC":
                misc_lo(step)
            elif step[0] == "S":
                row_max(*step[1:])
            elif step[0] == "T":
                probs_lo(*step[1:])

        def split_wm(c):
            dve.wait_ge(wm_hi, c + 1)
            u = (USE_WM + c) % 2
            dve.tensor_tensor(wm_l[c][:, :], raw[u][:, :], f32(wm_h[c][:, :]), ALU.subtract).then_inc(raw_split[u], 1)

        def y_gate(t):
            dve.wait_ge(ymT_ready, t + 1)
            if t >= 1:
                dve.wait_ge(ymlo_ready, t)
            dve.tensor_tensor(ymf[:, :, :], ps[:, 6 + t % 2, :].rearrange("p (c n) -> p c n", c=NC),
                              gmT[:, :, P * t:P * t + P], ALU.mult).then_inc(ymf_ready, 1)

        def y_lo(t):
            dve.wait_ge(ymhi_ready, t + 1)
            dve.tensor_tensor(ym_l[t % 2][:, :, :], ymf[:, :, :], f32(ym_h[t % 2][:, :, :]), ALU.subtract).then_inc(ymlo_ready, 1)

        def add_r(t):
            dve.wait_ge(r_ready, t + 1)
            dve.wait_ge(rstdr_ready, 1)
            dve.wait_ge(res_in[t % 4], 16 * (t // 4 + 1))
            dve.scalar_tensor_tensor(xres[t % 4][:, :], out_banks("R", t), rstd_r[:, t:t + 1],
                                     xres[t % 4][:, :], ALU.mult, ALU.add).then_inc(r_added, 1)

        def add_m(t):
            dve.wait_ge(m_ready, t + 1)
            dve.wait_ge(rstdm_ready, t + 1)
            dve.wait_ge(r_added, t + 1)
            dve.scalar_tensor_tensor(xres[t % 4][:, :], out_banks("M", t), rstd_m[:, t:t + 1],
                                     xres[t % 4][:, :], ALU.mult, ALU.add).then_inc(m_added, 1)

        def finish(t):
            dve.wait_ge(rstdo_ready, t + 1)
            if t == 0:
                dve.wait_ge(fg_in, 16)
            if t >= 2:
                dve.wait_ge(out_done[t % 2], 16 * (t // 2))
            dve.scalar_tensor_tensor(ost[t % 2][:, :], xres[t % 4][:, :], rstd_o[:, t:t + 1], fg_row[:, :], ALU.mult, ALU.mult)\
               .then_inc(o_ready, 1)

        for c in range(NC):
            if c == 0:
                y_gate(0)
            split_wm(c)
            if c == 0:
                y_lo(0)
        add_r(0)
        for t in range(NT):
            if t + 1 < NT:
                y_gate(t + 1)
                y_lo(t + 1)
                add_r(t + 1)
            if t >= 1:
                finish(t - 1)
            add_m(t)
        finish(NT - 1)

    @block.gpsimd
    def _(pool):
        own = [0]

        def after(ins):
            own[0] += 1
            ins.then_inc(pool_own, 1)
            pool.wait_ge(pool_own, own[0])

        def rstd(dst, ssq, n, scale, ready):
            if scale is None:
                after(pool.tensor_tensor(dst, ssq, inv_n[:, :], ALU.mult))
                after(pool.tensor_scalar(dst, dst, 1.0, EPS, ALU.mult, ALU.add))
            else:
                after(pool.tensor_scalar(dst, ssq, scale, EPS, ALU.mult, ALU.add))
            pool.tensor_tensor(dst, dst, minus_half[:, 0:n], ALU.pow).then_inc(ready, 1)

        def split(hi, lo, src, hi_sem, count):
            pool.tensor_scalar(hi, src, 1.0, 0.0, ALU.mult, ALU.add).then_inc(hi_sem, 1)
            pool.wait_ge(hi_sem, count)
            return pool.tensor_tensor(lo, src, f32(hi), ALU.subtract)

        def split_chunk(c):
            use = USE_CHUNK + c
            s, v = raw_landed(use)
            pool.wait_ge(s, v)
            if c >= 2:
                pool.wait_ge(z_ready, z_use(c - 2, 1) + 1)
            src = raw[use % 2][:, :].rearrange("p (k n) -> p k n", k=KD)
            split(cw_h[c % 2][:, :, :], cw_l[c % 2][:, :, :], src, cw_hi, c + 1).then_inc(raw_split[use % 2], 1)

        def rstd_x_of(t):
            pool.wait_ge(ssqx_ready, t + 1)
            rstd(rstd_x[:, t:t + 1], ssq_x[:, t:t + 1], 1, 1.0 / D, rstdx_ready)

        def rstd_z_of(t):
            pool.wait_ge(zstat_ready, t + 1)
            rstd(rstd_z[:, t, :], ssq_z[:, t, :], 2, None, rstdz_ready)

        pool.memset(gate_raw[:, :, :, :], 0.0).then_inc(zeroed, 1)
        pool.memset(inv_n[:, 0:1], 1.0 / QR)
        pool.memset(inv_n[:, 1:2], 1.0 / KVR)
        after(pool.memset(minus_half[:, :], -0.5))
        for i in range(NT + 2):
            if i < NT:
                rstd_x_of(i)
            if i == 5:
                split_chunk(0)
            if i == 7:
                split_chunk(1)
            if 2 <= i:
                rstd_z_of(i - 2)
        pool.wait_ge(latlo_ready, NT)
        pool.wait_ge(gates_in, 64)
        split(gw_h[:, :, :, :], gw_l[:, :, :, :], gate_raw, gw_hi, 1).then_inc(gw_ready, 1)

        def split_xr(c):
            pool.wait_ge(conv_done, c + 1)
            if c >= 1:
                pool.wait_ge(gate_ready, 4 * c)
            split(xr_h[:, :], xr_l[:, :], xr[c], xr_hi_done, c + 1).then_inc(xrs_ready, 1)

        def sum_squares(c):
            pool.wait_ge(hsq_ready, c + 1)
            if c >= 2:
                pool.wait_ge(hsq_summed, c - 1)
            pool.tensor_tensor(sq_sum[:, :], sq_sum[:, :], hsq[:, :], ALU.add).then_inc(hsq_summed, 1)

        for c in range(len(CHUNKS)):
            if c + 2 < len(CHUNKS):
                split_chunk(c + 2)
            if c < NC:
                split_xr(c)
            if 5 <= c < 4 + NC:
                sum_squares(c - 4)
        pool.wait_ge(yr_done, NC)
        for k in range(3):
            use = USE_Q + k
            s, v = raw_landed(use)
            pool.wait_ge(s, v)
            if k < 2:
                hi, lo = wq_h[:, k, :, :], wq_l[:, k, :, :]
            else:
                hi, lo = wkv_h[:, :], wkv_l[:, :]
            src = raw[use % 2][:, :]
            if k < 2:
                src = src.rearrange("p (h n) -> p h n", h=H)
            split(hi, lo, src, aw_hi, k + 1).then_inc(raw_split[use % 2], 1)
        pool.wait_ge(ssr_copied, 1)
        rstd(rstd_r[:, :], ssq_r[:, :], NT, 1.0 / RNN, rstdr_ready)

        pool.wait_ge(rstdr_ready, 1)
        for h in range(H):
            for half in range(2):
                u = 2 * h + half
                c = slice(HALF * half, HALF * half + HALF)
                if u >= 1:
                    pool.wait_ge(q_ready, u)
                if u == 2:
                    pool.wait_ge(krope_copied, 6)
                pool.wait_ge(qrot_ready, u + 1)
                split(qh[64:96, c], ql[64:96, c], qt[1][64:96, :], qrope_hi, u + 1).then_inc(q_ready, 1)
            if h == 0:
                pool.wait_ge(krope_ready, 1)
                pool.wait_ge(q_ready, 2)
                for i in range(1, 4):
                    for kk in (kh, kl):
                        pool.tensor_scalar(kk[64:96, i, :], f32(kk[64:96, 0, :]), 1.0, 0.0, ALU.mult, ALU.add)\
                            .then_inc(krope_copied, 1)
        pool.wait_ge(misc_ready, misc_no[("Q", H - 1, 1)] + 1)
        pool.wait_ge(s_ready, s_no[("S", 5, 7)] + 1)
        pool.wait_ge(q_ready, 2 * H)
        for c in range(NC):
            use = USE_WR + c
            s, v = raw_landed(use)
            pool.wait_ge(s, v)
            split(wr_h[c][:, :], wr_l[c][:, :], raw[use % 2][:, :], wr_hi, c + 1).then_inc(raw_split[use % 2], 1)
            split(yr_h[c][:, :], yr_l[c][:, :], yrT[:, c, :], yr_hi_done, c + 1).then_inc(yr_lo, 1)
        for t in range(NT):
            pool.wait_ge(ssm_ready, t + 1)
            rstd(rstd_m[:, t:t + 1], ssq_m[:, t:t + 1], 1, 1.0 / (H * VD), rstdm_ready)
            if t >= 4:
                pool.wait_ge(sso_ready, t - 3)
                rstd(rstd_o[:, t - 4:t - 3], ssq_o[:, t - 4:t - 3], 1, 1.0 / D, rstdo_ready)
        for t in range(NT - 4, NT):
            pool.wait_ge(sso_ready, t + 1)
            rstd(rstd_o[:, t:t + 1], ssq_o[:, t:t + 1], 1, 1.0 / D, rstdo_ready)

    ctx.close()


_INS = ["x", "norm_in_g", "w_in", "q_norm_g", "w_q_b", "kv_norm_g", "w_kv_b", "conv_w", "conv_b", "w_rg_a",
        "b_rg_a", "w_rg_x", "b_rg_x", "lru_param", "out_norm_mla_g", "out_norm_rnn_g", "w_out", "final_norm_g"]


def _constants():
    import numpy as np

    eye = np.eye(P, dtype=np.float32)
    pos = np.arange(SEQ, dtype=np.float32)
    inv_freq = np.float32(10000.0) ** (-np.arange(0, ROPE, 2, dtype=np.float32) / np.float32(ROPE))
    ang = (pos[:, None] * inv_freq[None, :].astype(np.float32)).astype(np.float32)
    cos, sin = np.cos(ang).T, np.sin(ang).T
    trig = np.concatenate([cos, cos, -sin, sin]).astype(np.float32)
    return {"ident": eye, "stack": np.concatenate([eye[:VD, :VD], eye[:VD, :VD]]), "trig": trig}


def kernel(**inputs):
    import numpy as _np
    import concourse.bacc as _bacc
    from concourse import mybir as _mybir
    from concourse.bass_utils import run_bass_kernel_spmd as _run

    nc = _bacc.Bacc("TRN2", target_bir_lowering=False, num_devices=1)
    arrays, args = {}, {}
    for name, value in [(n, inputs[n]) for n in _INS] + list(_constants().items()):
        v = _np.ascontiguousarray(value)
        arrays[f"in_{name}_dram"] = v
        args[name] = nc.dram_tensor(f"in_{name}_dram", v.shape, _mybir.dt.from_np(v.dtype), kind="ExternalInput").ap()
    out = nc.dram_tensor("out_0_dram", (1, SEQ, D), _mybir.dt.float32, kind="ExternalOutput").ap()
    build(nc, args, out)
    r = _run(nc, [arrays], core_ids=[0])
    return r.results[0]["out_0_dram"]
```

```python
import concourse.bass as bass
from concourse import mybir

F32 = mybir.dt.float32
F32R = mybir.dt.float32r
BF16 = mybir.dt.bfloat16
ALU = mybir.AluOpType
ACT = mybir.ActivationFunctionType
AX = mybir.AxisListType

P = 128
SEQ, D = 1024, 1024
NT = SEQ // P
KD = D // P
HALF = 512
H, NOPE, ROPE, VD = 8, 64, 32, 64
QK = NOPE + ROPE
QR, KVR = 256, 128
LAT = QR + KVR + ROPE
RNN = 512
NC = RNN // P
EPS = 1e-6
SCALE = float(QK) ** -0.5
MASKED = -2.0 ** 127

COL_GM, COL_X, COL_GR = LAT, LAT + RNN, LAT + 2 * RNN
CHUNKS = [("x", c, COL_X + P * c) for c in range(NC)] + \
         [("gr", c, COL_GR + P * c) for c in range(NC)] + \
         [("gm", c, COL_GM + P * c) for c in range(NC)]


SLOT_S = (3.5, 4, 4, 6.5, 8, 9.5, 10, 11.5)
SLOT_Q = (-2, 2)
SLOT_K = (3.5, 8)
SLOT_C = (0.5, 5.5)
SLOT_V = (6.5, 8.5, 9.5, 11.5)
SLOT_LAST_V = 0.5
SLOT_R = (1.5, 3.5, 3.5, 4, 7.5, 11.5)
SLOT_W = (-4, -1.5)
OUT_W = (0, 1)


def attention_steps():
    steps = [("Q", 0, 0), ("Q", 0, 1), ("K", 0, 0), ("K", 0, 1)]
    steps += [("V", 0, 0), ("V", 0, 1), ("S", 0, 0), ("S", 0, 1), ("S", 0, 2),
              ("S", 0, 3), ("Q", 1, 0), ("S", 0, 4), ("S", 0, 5), ("V", 0, 2)]
    slots = [[] for _ in range(24 * H)]

    def put(h, slot, step):
        slots[max(0, int(2 * (12 * h + slot)))] += [step]

    for h in range(H):
        if h:
            put(h, SLOT_C[0], ("C", 2 * h - 1))
        put(h, SLOT_C[1], ("C", 2 * h))
        if h + 1 < H:
            for half in range(0 if h else 1, 2):
                put(h, SLOT_Q[half], ("Q", h + 1, half))
            for t in range(NT):
                put(h, SLOT_S[t], ("S", h + 1, t))
        if h % 2 == 0 and h + 2 < H:
            for half in range(2):
                put(h, SLOT_K[half], ("K", h // 2 + 1, half))
    for i, slot in enumerate(SLOT_R):
        put(H - 1, slot, ("R", i // NC, i % NC))
    for slot, w in zip(SLOT_W, OUT_W):
        put(H - 1, slot, ("W", w))
    put(0, SLOT_LAST_V, ("V", 0, 3))
    for p in range(4):
        put(3, SLOT_V[p], ("V", 1, p))
    transposes = [("T", n, j) for n in range(2 * H) for j in range(4 + 4 * (n % 2))]
    steps += transposes[:1] + [("S", 0, 6)] + transposes[1:2] + [("S", 0, 7)]
    for u, (_, n, j) in enumerate(transposes):
        steps += transposes[u + 2:u + 3] + slots[2 * u] + [("PV", n, j)]
        if j == 3 + 4 * (n % 2):
            steps += [("Y", n)]
        steps += slots[2 * u + 1]
    return steps + [("C", 2 * H - 1)]


def scores_after_transposes(steps):
    start = steps.index(("T", 0, 0))
    order, held = steps[:start], []
    for step in steps[start:]:
        if step[0] == "S":
            held += [step]
        else:
            order += [step]
            if step[0] == "T":
                order += held
                held = []
    return order + held


def build(nc, a, out):
    KB = 1024
    base = (nc.sbuf_base + 31) // 32 * 32

    def at(name, shape, off, dt=F32):
        return nc.alloc_sbuf_tensor_at(name, shape, dt, offset=base + int(off))

    off = [0]

    def small(name, shape, dt=F32):
        n = 4 if dt != BF16 else 2
        for s in shape[1:]:
            n *= s
        t = at(name, shape, off[0], dt)
        off[0] += (n + 31) // 32 * 32
        return t

    trig = small("trig", [P, SEQ])
    ident = small("ident", [P, P])
    stack = small("stack", [P, VD])
    one_col = small("one_col", [P, 1])
    half_rows = small("half_rows", [1, P], BF16)
    masked = small("masked", [1, VD], BF16)
    g_mla = small("g_mla", [P, NC])
    g_rnn = small("g_rnn", [P, NC])
    conv_w = small("conv_w", [P, 4, NC])
    conv_b = small("conv_b", [P, NC])
    bias_a = small("bias_a", [P, NC])
    bias_x = small("bias_x", [P, NC])
    lru = small("lru", [P, NC])
    sp = small("sp", [P, 12, NC])
    sp8 = small("sp8", [P, NC])
    sp16 = small("sp16", [P, NC])
    inv_n = small("inv_n", [P, 2])
    minus_half = small("minus_half", [P, NT])
    ssq_x = small("ssq_x", [P, NT])
    rstd_x = small("rstd_x", [P, NT])
    ssq_z = small("ssq_z", [P, NT, 2])
    rstd_z = small("rstd_z", [P, NT, 2])
    ssq_r = small("ssq_r", [P, NT])
    rstd_r = small("rstd_r", [P, NT])
    ssq_m = small("ssq_m", [P, NT])
    rstd_m = small("rstd_m", [P, NT])
    ssq_o = small("ssq_o", [P, NT + 1])
    rstd_o = small("rstd_o", [P, NT])
    nmax = small("nmax", [P, H * NT])
    rsum = small("rsum", [P, H * NT])
    rinv = small("rinv", [P, H * NT])
    assert off[0] <= 7.5 * KB, off[0]
    B0 = 7.5 * KB
    latT_h = at("latT_h", [P, 3, SEQ], B0, F32R)
    latT_l = at("latT_l", [P, 3, SEQ], B0 + 12 * KB, F32R)
    gmT = at("gmT", [P, NC, SEQ], B0 + 24 * KB)
    yrT = at("yrT", [P, NC, SEQ], B0 + 40 * KB)
    raw = [at(f"raw{i}", [P, 1024], B0 + (56 + 4 * i) * KB) for i in range(2)]
    R1 = B0 + 64 * KB
    R2 = R1 + 50.5 * KB
    lat_w_h = at("lat_w_h", [P, KD, LAT], R1, F32R)
    lat_w_l = at("lat_w_l", [P, KD, LAT], R1 + 13 * KB, F32R)
    xst = [at(f"xst{i}", [P, D], R1 + (26 + 4 * i) * KB) for i in range(3)]
    g_in_row = at("g_in_row", [P, D], R1 + 38 * KB)
    g_lat_row = at("g_lat_row", [P, QR + KVR], R1 + 42 * KB)
    latn = [at(f"latn{i}", [P, QR + KVR], R1 + (43.5 + 1.5 * i) * KB) for i in range(2)]
    krs = [at(f"krs{i}", [P, P], R1 + (46.5 + 0.5 * i) * KB) for i in range(2)]
    rope_t = at("rope_t", [P, P], R1 + 47.5 * KB)
    hT_h = at("hT_h", [P, KD, SEQ], R2, F32R)
    hT_l = at("hT_l", [P, KD, SEQ], R2 + 32 * KB, F32R)
    cw_h = [at(f"cw_h{i}", [P, KD, P], R2 + (64 + 4 * i) * KB, F32R) for i in range(2)]
    cw_l = [at(f"cw_l{i}", [P, KD, P], R2 + (72 + 4 * i) * KB, F32R) for i in range(2)]
    kpe = at("kpe", [P, SEQ], R2 + 80 * KB)
    lat_raw = [at(f"lat_raw{k}", [P, 2, LAT], o) for k, o in
               enumerate((B0 + 56 * KB, B0 + 60 * KB, R2 + 64 * KB, R2 + 68 * KB))]
    junk = [gmT[:, c, :] for c in (0, 2, 3)]
    gate_raw = gmT[:, 1:2, :].rearrange("p a (g c n) -> p (a g) c n", g=2, c=NC)
    xr = [gmT[:, c, :] for c in range(NC)]
    hsq = at("hsq", [P, SEQ], R1)
    xr_h = at("xr_h", [P, SEQ], R1 + 8 * KB, F32R)
    xr_l = at("xr_l", [P, SEQ], R1 + 12 * KB, F32R)
    ra = at("ra", [P, SEQ], R1 + 16 * KB)
    iu = at("iu", [P, SEQ], R1 + 20 * KB)
    mh = at("mh", [P, SEQ], R1 + 24 * KB)
    gw_h = at("gw_h", [P, 2, NC, P], R1 + 28 * KB, F32R)
    gw_l = at("gw_l", [P, 2, NC, P], R1 + 32 * KB, F32R)
    xpad = at("xpad", [P, SEQ + 4], R1 + 36 * KB)
    sg = [at(f"sg{i}", [P, HALF], R1 + (40.25 + 2 * i) * KB) for i in range(2)]
    sq_sum = at("sq_sum", [P, SEQ], R1 + 44.25 * KB)
    kr_h = at("kr_h", [P, SEQ], R1 + 44.25 * KB, F32R)
    kr_l = at("kr_l", [P, SEQ], R2 + 80 * KB, F32R)
    wq_h = at("wq_h", [P, 2, H, P], R1, F32R)
    wq_l = at("wq_l", [P, 2, H, P], R1 + 8 * KB, F32R)
    wkv_h = at("wkv_h", [P, 2 * H * VD], R1 + 16 * KB, F32R)
    wkv_l = at("wkv_l", [P, 2 * H * VD], R1 + 20 * KB, F32R)
    qh = at("qh", [P, SEQ], R1 + 24 * KB, F32R)
    ql = at("ql", [P, SEQ], R1 + 28 * KB, F32R)
    qc = [at(f"qc{i}", [P, HALF], R1 + (32 + 2 * i) * KB) for i in range(2)]
    qn = at("qn", [P, HALF], R1 + 38 * KB)
    ptl = [at(f"ptl{i}", [P, HALF], o, F32R) for i, o in enumerate((R1 + 40.25 * KB, R1 + 42.25 * KB, R1 + 36 * KB))]
    pth = [at(f"pth{i}", [P, HALF], o, F32R) for i, o in enumerate((R1 + 44.25 * KB, R1 + 46.25 * KB, R2 + 82 * KB))]
    yTs = at("yTs", [P, HALF], R1 + 48.25 * KB)
    kh = at("kh", [P, 4, SEQ], R2, F32R)
    kl = at("kl", [P, 4, SEQ], R2 + 16 * KB, F32R)
    ynat = at("ynat", [P, NT, NC * P], R2 + 32 * KB)
    vv = at("vv", [P, NT, 4, P], R2 + 48 * KB, F32R)
    probs = [at(f"probs{t}", [P, P * (t + 1)], R2 + 64 * KB + 2 * P * t * (t + 1)) for t in range(NT)]
    slot4 = [B0, B0 + 4 * KB, B0 + 8 * KB, B0 + 12 * KB, R1, R1 + 4 * KB, R1 + 8 * KB, R1 + 12 * KB]
    wr_h = [at(f"wr_h{c}", [P, D], slot4[c], F32R) for c in range(NC)]
    wr_l = [at(f"wr_l{c}", [P, D], slot4[4 + c], F32R) for c in range(NC)]
    yr_h = [at(f"yr_h{c}", [P, SEQ], R2 + (0, 4, 16, 20)[c] * KB, F32R) for c in range(NC)]
    yr_l = [at(f"yr_l{c}", [P, SEQ], B0 + (40 + 4 * c) * KB, F32R) for c in range(NC)]
    wm_h = [at(f"wm_h{c}", [P, D], o, F32R) for c, o in
            enumerate((R1 + 24 * KB, R1 + 28 * KB, R1 + 32 * KB, R2 + 8 * KB))]
    wm_l = [at(f"wm_l{c}", [P, D], o, F32R) for c, o in
            enumerate((B0 + 16 * KB, B0 + 20 * KB, R1 + 16 * KB, R1 + 20 * KB))]
    xres = [at(f"xres{i}", [P, D], R2 + (64 + 4 * i) * KB) for i in range(4)]
    ost = [at("ost0", [P, D], R2 + 80 * KB), at("ost1", [P, D], R2 + 48 * KB)]
    unused_sq = [at(f"unused_sq{i}", [P, D], R2 + (52 + 4 * i) * KB) for i in range(3)]
    fg_row = at("fg_row", [P, D], R2 + 12 * KB)
    ymf = at("ymf", [P, NC, P], R2 + 24 * KB)
    ym_h = [at(f"ym_h{i}", [P, NC, P], R2 + (26 + i) * KB + i * KB, F32R) for i in range(2)]
    ym_l = [at("ym_l0", [P, NC, P], R2 + 30 * KB, F32R), at("ym_l1", [P, NC, P], R1 + 48.25 * KB, F32R)]
    assert base + R2 + 84 * KB <= nc.sbuf_usable_end, (base, R2, nc.sbuf_usable_end)

    ps = nc.alloc_psum_tensor("ps", [P, 8, HALF], F32)

    def f32(ap):
        return ap.bitcast(F32)

    from contextlib import ExitStack
    ctx = ExitStack()

    def sem(name):
        return ctx.enter_context(nc.semaphore(name))

    first_in = sem("first_in")
    ident_in = sem("ident_in")
    const_in = sem("const_in")
    gates_in = sem("gates_in")
    x_in = [sem(f"x_in{i}") for i in range(3)]
    lat_in = [sem(f"lat_in{k}") for k in range(4)]
    latw_lo = sem("latw_lo")
    raw_in = [sem(f"raw_in{i}") for i in range(2)]
    raw_split = [sem(f"raw_split{i}") for i in range(2)]
    res_in = [sem(f"res_in{i}") for i in range(4)]
    fg_in = sem("fg_in")
    out_done = [sem(f"out_done{i}") for i in range(2)]
    zeroed = sem("zeroed")
    dve_own = sem("dve_own")
    pool_own = sem("pool_own")
    lru_exp = sem("lru_exp")
    sp_in = sem("sp_in")
    sp_ready = sem("sp_ready")
    ssqx_ready = sem("ssqx_ready")
    rstdx_ready = sem("rstdx_ready")
    h_ready = sem("h_ready")
    xT_ready = sem("xT_ready")
    hhi_ready = sem("hhi_ready")
    hlo_ready = sem("hlo_ready")
    latw_hi = sem("latw_hi")
    z_ready = sem("z_ready")
    zstat_ready = sem("zstat_ready")
    rstdz_ready = sem("rstdz_ready")
    latn_ready = sem("latn_ready")
    latT_ready = sem("latT_ready")
    lathi_ready = sem("lathi_ready")
    kpe_half = sem("kpe_half")
    latlo_ready = sem("latlo_ready")
    cw_hi = sem("cw_hi")
    gw_hi = sem("gw_hi")
    gw_ready = sem("gw_ready")
    xr_hi_done = sem("xr_hi_done")
    xpad_ready = sem("xpad_ready")
    conv_done = sem("conv_done")
    xrs_ready = sem("xrs_ready")
    gate_ready = sem("gate_ready")
    sig_ready = sem("sig_ready")
    exp_ready = sem("exp_ready")
    min_ready = sem("min_ready")
    sqrt_ready = sem("sqrt_ready")
    scan_done = sem("scan_done")
    hsq_ready = sem("hsq_ready")
    hsq_summed = sem("hsq_summed")
    sg_ready = sem("sg_ready")
    gate_done = sem("gate_done")
    yr_done = sem("yr_done")
    ssr_ready = sem("ssr_ready")
    ssr_copied = sem("ssr_copied")
    aw_hi = sem("aw_hi")
    krope_hi = sem("krope_hi")
    krope_ready = sem("krope_ready")
    krope_copied = sem("krope_copied")
    misc_ready = sem("misc_ready")
    mhi_ready = sem("mhi_ready")
    misc_done = sem("misc_done")
    qc_ready = sem("qc_ready")
    qrope_hi = sem("qrope_hi")
    q_ready = sem("q_ready")
    s_ready = sem("s_ready")
    max_ready = sem("max_ready")
    p_ready = sem("p_ready")
    pt_ready = sem("pt_ready")
    pthi_ready = sem("pthi_ready")
    ptlo_ready = sem("ptlo_ready")
    pv_done = sem("pv_done")
    yT_copied = sem("yT_copied")
    w_out_hi = sem("w_out_hi")
    w_act_hi = sem("w_act_hi")
    yr_hi_done = sem("yr_hi_done")
    yr_lo = sem("yr_lo")
    ssm_ready = sem("ssm_ready")
    rstdm_ready = sem("rstdm_ready")
    rstdr_ready = sem("rstdr_ready")
    ymT_ready = sem("ymT_ready")
    ymf_ready = sem("ymf_ready")
    ymhi_ready = sem("ymhi_ready")
    ymlo_ready = sem("ymlo_ready")
    r_ready = sem("r_ready")
    r_added = sem("r_added")
    m_ready = sem("m_ready")
    m_added = sem("m_added")
    sso_ready = sem("sso_ready")
    rstdo_ready = sem("rstdo_ready")
    o_ready = sem("o_ready")

    w_in = a["w_in"][0].rearrange("(k p) n -> p k n", p=P)
    w_out = a["w_out"][0].rearrange("(k p) n -> p k n", p=P)
    w_q = a["w_q_b"][0].rearrange("(k p) (h e) -> p k h e", p=P, h=H)
    w_kv = a["w_kv_b"][0].rearrange("p (h two d) -> p two h d", two=2, d=VD)
    x_t = a["x"][0].rearrange("(t p) d -> t p d", p=P)
    out_t = out[0].rearrange("(t p) d -> t p d", p=P)

    USE_CHUNK = 0
    USE_Q, USE_KV = USE_CHUNK + len(CHUNKS), USE_CHUNK + len(CHUNKS) + 2
    USE_WR, USE_WM = USE_KV + 1, USE_KV + 1 + NC
    raw_parts = {}
    raw_parts[USE_Q] = raw_parts[USE_Q + 1] = 3
    raw_parts[USE_KV] = 2

    def raw_landed(use):
        return raw_in[use % 2], 16 * sum(raw_parts.get(u, 1) for u in range(use % 2, use + 1, 2))

    def split_of(use):
        return raw_split[use % 2], use // 2 + 1

    def passes(hi_a, lo_a, hi_b, lo_b):
        return ((hi_a, hi_b), (hi_a, lo_b), (lo_a, hi_b))

    def z_bank(m):
        return ps[:, 4 + m % 4, :]

    def z_use(c, half):
        return NT + 2 * c + half

    steps = attention_steps()
    MISC = [s for s in steps if s[0] in "VKQC"]
    FIRST_MISC = 6
    misc_no = {s: i for i, s in enumerate(MISC)}
    s_no = {s: i for i, s in enumerate(s for s in steps if s[0] == "S")}
    t_no = {("T",) + s[1:]: i for i, s in enumerate(s for s in steps if s[0] == "T")}

    def misc_bank(i):
        return (1, 2, 4, 5, 6, 7)[i] if i < FIRST_MISC else 7

    def misc_before(i):
        return 0 if i < FIRST_MISC else i

    SCORE_BANK = (0, 1, 2, 3, 0, 2, 0, 2)

    def scores_before(h, t):
        return max(0, NT * h + (-1, -1, 0, 0, 2, 4, 5, 6)[t])

    def tile_scores(t):
        b = SCORE_BANK[t]
        return ps[:, b:b + 2, :].rearrange("p b n -> p (b n)")[:, 0:P * (t + 1)] if t >= 4 else ps[:, b, 0:P * (t + 1)]

    def query_tiles(n, j):
        return max(0, j - 4 * (n % 2))

    uses = [("R", 0)] + [u for t in range(NT) for u in ([("R", t + 1)] if t + 1 < NT else []) + [("M", t)]]

    def out_banks(kind, t):
        b = 2 * (uses.index((kind, t)) % 3)
        return ps[:, b:b + 2, :].rearrange("p b n -> p (b n)")

    def out_columns(t):
        return [slice(0, D)] if t < NT - 1 else [slice(0, HALF), slice(HALF, D)]

    block = ctx.enter_context(nc.Block())

    @block.sync
    def _(sp_):
        def load(t, src, s):
            sp_.dma_start(t, src).then_inc(s, 16)

        def x_load(t):
            if t >= 3:
                sp_.wait_ge(xT_ready, 2 * (t - 3) + 2)
            load(xst[t % 3][:, :], x_t[t], x_in[t % 3])

        def raw_load(use):
            dst = raw[use % 2]
            if use < 2:
                sp_.wait_ge(latw_lo, use + 1)
            else:
                sp_.wait_ge(*split_of(use - 2))
            s = raw_in[use % 2]
            if use < USE_Q:
                col = CHUNKS[use - USE_CHUNK][2]
                load(dst[:, :].rearrange("p (k n) -> p k n", k=KD), w_in[:, :, col:col + P], s)
            elif use < USE_KV:
                k = use - USE_Q
                d = dst[:, :].rearrange("p (h n) -> p h n", h=H)
                load(d[:, :, 0:QK], w_q[:, k, :, :], s)
                load(d[:, :, QK:QK + 16], w_q[:, k, :, NOPE + 16:QK], s)
                load(d[:, :, QK + 16:P], w_q[:, k, :, NOPE:NOPE + 16], s)
            elif use == USE_KV:
                d = dst[:, :].rearrange("p (two h d) -> p two h d", two=2, h=H)
                load(d[:, 0, :, :], w_kv[:, 0, :, :], s)
                load(d[:, 1, :, :], w_kv[:, 1, :, :], s)
            elif use < USE_WM:
                load(dst[:, :], w_out[:, NC + use - USE_WR, :], s)
            else:
                load(dst[:, :], w_out[:, use - USE_WM, :], s)

        def latent_load(k):
            load(lat_raw[k][:, :, :], w_in[:, 2 * k:2 * k + 2, 0:LAT], lat_in[k])

        x_load(0)
        load(g_in_row[:, :], a["norm_in_g"].to_broadcast((P, D)), first_in)
        load(ident[:, :], a["ident"], ident_in)
        for k in range(4):
            latent_load(k)
        x_load(1)
        load(g_lat_row[:, 0:QR], a["q_norm_g"].to_broadcast((P, QR)), const_in)
        load(g_lat_row[:, QR:], a["kv_norm_g"].to_broadcast((P, KVR)), const_in)
        x_load(2)
        load(trig[NOPE:P, :], a["trig"], const_in)
        load(stack[:, :], a["stack"], const_in)
        with nc.allow_non_contiguous_dma(reason="a few per-channel parameters"):
            for t, name in ((g_mla, "out_norm_mla_g"), (g_rnn, "out_norm_rnn_g"), (conv_b, "conv_b"),
                            (bias_a, "b_rg_a"), (bias_x, "b_rg_x"), (lru, "lru_param")):
                load(t[:, :], a[name][0].rearrange("(c p) -> p c", p=P), const_in)
            load(conv_w[:, :, :], a["conv_w"][0].rearrange("k (c p) -> p k c", p=P), const_in)
        sp_.wait_ge(zeroed, 1)
        for g, name in enumerate(("w_rg_a", "w_rg_x")):
            w = a[name][0].rearrange("(c two) i j -> two i c j", two=2)
            for b in range(2):
                load(gate_raw[64 * b:64 * b + 64, g, :, 64 * b:64 * b + 64], w[b], gates_in)
        x_load(3)
        raw_load(0)
        x_load(4)
        raw_load(1)
        for t in range(5, NT):
            x_load(t)
        for use in range(2, USE_WR + 2):
            raw_load(use)
        for use in range(USE_WR + 2, USE_WM + NC):
            raw_load(use)
        sp_.wait_ge(pv_done, len(t_no))
        load(fg_row[:, :], a["final_norm_g"].rearrange("(o d) -> o d", o=1).to_broadcast((P, D)), fg_in)
        for t in range(4):
            load(xres[t][:, :], x_t[t], res_in[t])
        for t in range(NT):
            for n, c in enumerate(out_columns(t)):
                sp_.wait_ge(o_ready, t + 1 + n)
                load(out_t[t][:, c], ost[t % 2][:, c], out_done[t % 2])
            if t + 4 < NT:
                load(xres[t % 4][:, :], x_t[t + 4], res_in[t % 4])
        for i in range(2):
            sp_.wait_ge(out_done[i], 16 * sum(len(out_columns(t)) for t in range(i, NT, 2)))

    N_CONST = 2 + 2 + 6 + 1

    @block.tensor
    def _(pe):
        def transpose_h(t):
            pe.wait_ge(h_ready, t + 1)
            for b in range(2):
                if t >= 1:
                    pe.wait_ge(hlo_ready, 2 * (t - 1) + b + 1)
                for k in range(4):
                    mm = pe.transpose(ps[:, b, P * k:P * k + P], xst[t % 3][:, P * (4 * b + k):P * (4 * b + k) + P], ident[:, :])
                mm.then_inc(xT_ready, 1)

        def z_free(m):
            if m < 4:
                return
            u = m - 4
            if u < NT:
                pe.wait_ge(latn_ready, u + 1)
            else:
                kind, c, _ = CHUNKS[(u - NT) // 2]
                if kind == "x":
                    pe.wait_ge(xpad_ready, u - NT + 1)
                else:
                    pe.wait_ge(gate_done, u - NT - 2 * NC + 1)

        def latents(t):
            z_free(t)
            for b in range(2):
                pe.wait_ge(hlo_ready, 2 * t + b + 1)
                for k in range(4 * b, 4 * b + 4):
                    if t == 0 and k % 2 == 0:
                        pe.wait_ge(latw_lo, k // 2 + 1)
                    for n, (l, r) in enumerate(passes(hT_h, hT_l, lat_w_h, lat_w_l)):
                        mm = pe.matmul(z_bank(t)[:, 0:LAT], l[:, k, P * t:P * t + P], r[:, k, :],
                                       start=(k == 0 and n == 0), stop=(k == KD - 1 and n == 2))
            mm.then_inc(z_ready, 1)

        def transpose_latents(t):
            pe.wait_ge(latn_ready, t + 1)
            pe.wait_ge(zstat_ready, t + 1)
            if t >= 1:
                pe.wait_ge(latlo_ready, t)
            for k in range(3):
                pe.transpose(ps[:, 2, P * k:P * k + P], latn[t % 2][:, P * k:P * k + P], ident[:, :])
            pe.transpose(ps[:, 2, 3 * P:4 * P], krs[t % 2][:, :], ident[:, :]).then_inc(latT_ready, 1)

        def chunk(c, half):
            if half == 0:
                pe.wait_ge(*split_of(USE_CHUNK + c))
            m = z_use(c, half)
            z_free(m)
            for k in range(KD):
                for n, (l, r) in enumerate(passes(cw_h[c % 2], cw_l[c % 2], hT_h, hT_l)):
                    mm = pe.matmul(z_bank(m), l[:, k, :], r[:, k, HALF * half:HALF * half + HALF],
                                   start=(k == 0 and n == 0), stop=(k == KD - 1 and n == 2))
            mm.then_inc(z_ready, 1)

        def gates(c):
            if c == 0:
                pe.wait_ge(gw_ready, 1)
            pe.wait_ge(xrs_ready, c + 1)
            for g in range(2):
                for half in range(2):
                    u = 4 * c + 2 * g + half
                    if u >= 4:
                        pe.wait_ge(sig_ready, u - 3)
                    elif u == 0:
                        pe.wait_ge(latlo_ready, NT)
                    for n, (l, r) in enumerate(passes(gw_h, gw_l, xr_h, xr_l)):
                        mm = pe.matmul(ps[:, u % 4, :], l[:, g, c, :], r[:, HALF * half:HALF * half + HALF],
                                       start=(n == 0), stop=(n == 2))
                    mm.then_inc(gate_ready, 1)

        pe.wait_ge(ident_in, 16)
        transpose_h(0)
        for t in range(NT):
            if 1 <= t < NT - 1:
                transpose_h(t + 1)
            latents(t)
            if t == 0:
                transpose_h(1)
            if t >= 1:
                transpose_latents(t - 1)
        def misc(step):
            i = misc_no[step]
            if misc_before(i):
                pe.wait_ge(misc_done, misc_before(i))
                queries = sum(s[0] == "Q" for s in MISC[:misc_before(i)])
                if queries:
                    pe.wait_ge(qc_ready, queries)
            if 2 <= i < 6:
                pe.wait_ge(gate_done, 4 * NC - 5 + i)
            bank = ps[:, misc_bank(i), :]
            kind = step[0]
            if i == 0:
                pe.wait_ge(*split_of(USE_Q))
                pe.wait_ge(*split_of(USE_Q + 1))
            if i == 2:
                pe.wait_ge(*split_of(USE_KV))
            if kind == "V":
                _, half, part = step
                for jj in range(2):
                    j = 2 * part + jj
                    for n, (l, r) in enumerate(passes(latT_h, latT_l, wkv_h, wkv_l)):
                        mm = pe.matmul(bank[:, 256 * jj:256 * jj + 256], l[:, 2, P * j:P * j + P],
                                       r[:, 512 + 256 * half:768 + 256 * half], start=(n == 0 and jj == 0), stop=(n == 2),
                                       skip_group_check=True)
            elif kind == "K":
                _, pair, half = step
                for n, (l, r) in enumerate(passes(wkv_h, wkv_l, latT_h, latT_l)):
                    mm = pe.matmul(bank, l[:, P * pair:P * pair + P], r[:, 2, HALF * half:HALF * half + HALF],
                                   start=(n == 0), stop=(n == 2))
            elif kind == "Q":
                _, h, half = step
                for k in range(2):
                    for n, (l, r) in enumerate(passes(wq_h, wq_l, latT_h, latT_l)):
                        mm = pe.matmul(bank, l[:, k, h, :], r[:, k, HALF * half:HALF * half + HALF],
                                       start=(k == 0 and n == 0), stop=(k == 1 and n == 2))
            else:
                _, n_item = step
                pe.wait_ge(yT_copied, n_item + 1)
                for tt in range(4):
                    mm = pe.matmul(bank[:, VD * tt:VD * tt + VD], yTs[:, P * tt:P * tt + P], stack[:, :],
                                   start=(tt == 0), stop=True, skip_group_check=True)
            mm.then_inc(misc_ready, 1)

        def scores(h, t):
            k = s_no[("S", h, t)]
            pe.wait_ge(q_ready, 2 * h + 1 + t // 4)
            pe.wait_ge(misc_done, misc_no[("K", h // 2, t // 4)] + 1)
            if h == 0:
                pe.wait_ge(krope_hi, 2)
                pe.wait_ge(krope_ready, 1)
            elif h < 4:
                pe.wait_ge(krope_copied, 2 * h)
            if scores_before(h, t):
                pe.wait_ge(p_ready, scores_before(h, t))
            elif t == 0:
                pe.wait_ge(ssr_copied, 1)
            n_keys = P * (t + 1)
            chunks = [(0, min(HALF, n_keys))] + ([(HALF, n_keys)] if n_keys > HALF else [])
            q0 = P * t
            b0 = SCORE_BANK[t]
            kslot = 2 * (h // 2 % 2) + h % 2
            for n, (q, ks) in enumerate(((qh, (kh, kl)), (ql, (kh,)))):
                for m, kk in enumerate(ks):
                    for c, (lo, hi) in enumerate(chunks):
                        mm = pe.matmul(ps[:, b0 + c, 0:hi - lo], q[0:QK, q0:q0 + P], kk[0:QK, kslot, lo:hi],
                                       start=(n == 0 and m == 0), stop=(n == 1), skip_group_check=True)
                if n == 0:
                    c = len(chunks) - 1
                    pe.matmul(ps[:, b0 + c, n_keys - 64 - chunks[c][0]:n_keys - chunks[c][0]], half_rows[:, :],
                              masked[:, :], start=False, stop=False, skip_group_check=True)
            mm.then_inc(s_ready, 1)

        def transpose_probs(n, j):
            h, g = divmod(n, 2)
            u = t_no[("T", n, j)]
            if j == 0:
                pe.wait_ge(p_ready, NT * h + 4 * g + 4)
            if u >= 2:
                pe.wait_ge(ptlo_ready, u - 1)
            elif u == 0:
                pe.wait_ge(misc_done, FIRST_MISC)
            for tt in range(query_tiles(n, j), 4):
                mm = pe.transpose(ps[:, 4 + u % 2, P * tt:P * tt + P], probs[4 * g + tt][:, P * j:P * j + P], ident[:, :])
            mm.then_inc(pt_ready, 1)

        def pv(n, j):
            h, g = divmod(n, 2)
            u = t_no[("T", n, j)]
            pe.wait_ge(ptlo_ready, u + 1)
            if j == 0:
                pe.wait_ge(misc_done, misc_no[("V", h // 4, 1 if g == 0 else 3)] + 1)
                if n >= 1:
                    pe.wait_ge(yT_copied, n)
            c0 = P * query_tiles(n, j)
            for m, pt in enumerate((pth, ptl)):
                mm = pe.matmul(ps[:, 6, c0:HALF], vv[:, j, h % 4, :], pt[u % 3][:, c0:HALF],
                               start=(j == 0 and m == 0), stop=(j == 4 * g + 3 and m == 1), skip_group_check=True)
            mm.then_inc(pv_done, 1)

        def project(kind, t, ys_h, ys_l, w_h, w_l, chunks=range(NC), halves=(0, 1)):
            i = uses.index((kind, t))
            if chunks[0] == 0 and i >= 3:
                k, tb = uses[i - 3]
                pe.wait_ge(r_added if k == "R" else m_added, tb + 1)
            elif chunks[0] == 0 and i < 2:
                pe.wait_ge(p_ready, H * NT - 1 + i)
            elif chunks[0] == 0:
                pe.wait_ge(ptlo_ready, len(t_no))
            b0 = 2 * (i % 3)
            for c in chunks:
                if kind == "R" and t == 0:
                    pe.wait_ge(*split_of(USE_WR + c))
                    pe.wait_ge(yr_lo, c + 1)
                if kind == "M" and t == 0:
                    pe.wait_ge(*split_of(USE_WM + c))
                for n, (l, r) in enumerate(passes(ys_h, ys_l, w_h, w_l)):
                    for half in halves:
                        mm = pe.matmul(ps[:, b0 + half, :], l(c), r[c][:, HALF * half:HALF * half + HALF],
                                       start=(c == 0 and n == 0), stop=(c == NC - 1 and n == 2), skip_group_check=True)
            if chunks[-1] == NC - 1:
                mm.then_inc(r_ready if kind == "R" else m_ready, 1)

        def project_r(t, chunks=range(NC)):
            project("R", t, lambda c: yr_h[c][:, P * t:P * t + P], lambda c: yr_l[c][:, P * t:P * t + P], wr_h, wr_l, chunks)

        def project_m(t):
            pe.wait_ge(ymlo_ready, t + 1)
            for halves in ((0, 1),) if t < NT - 1 else ((0,), (1,)):
                project("M", t, lambda c: ym_h[t % 2][:, c, :], lambda c: ym_l[t % 2][:, c, :], wm_h, wm_l, halves=halves)

        for c in range(len(CHUNKS)):
            chunk(c, 0)
            if c == 0:
                transpose_latents(NT - 1)
            if c == len(CHUNKS) - 1:
                pe.wait_ge(hsq_summed, NC - 1)
                pe.wait_ge(sig_ready, 4 * NC)
                for t in range(NT):
                    mm = pe.matmul(ps[:, 0, t:t + 1], sq_sum[:, P * t:P * t + P], one_col[:, :], start=True, stop=True)
                mm.then_inc(ssr_ready, 1)
                misc(steps[0])
                misc(steps[1])
            chunk(c, 1)
            if 3 <= c < 3 + NC:
                gates(c - 3)

        for step in steps[2:]:
            if step[0] in "VKQC":
                misc(step)
            elif step[0] == "S":
                scores(*step[1:])
            elif step[0] == "T":
                transpose_probs(*step[1:])
            elif step[0] == "PV":
                pv(*step[1:])
            elif step[0] == "R":
                project_r(step[1], [step[2]])

        def transpose_y(t):
            pe.wait_ge(misc_done, len(MISC))
            if t >= 2:
                pe.wait_ge(ymf_ready, t - 1)
            for b in range(NC):
                mm = pe.transpose(ps[:, 6 + t % 2, P * b:P * b + P], ynat[:, t, P * b:P * b + P], ident[:, :])
            mm.then_inc(ymT_ready, 1)

        transpose_y(0)
        for t in range(NT):
            if t + 1 < NT:
                transpose_y(t + 1)
                done = sum(s[:2] == ("R", t + 1) for s in steps)
                if done < NC:
                    project_r(t + 1, range(done, NC))
            project_m(t)

    @block.scalar
    def _(act):
        def split_latent_weights(k):
            act.wait_ge(lat_in[k], 16)
            act.activation(lat_w_h[:, 2 * k:2 * k + 2, :], lat_raw[k][:, :, :], ACT.Copy).then_inc(latw_hi, 1)

        def square_x(t):
            act.wait_ge(x_in[t % 3], 16 * (t // 3 + 1))
            if t >= 3:
                act.wait_ge(ssqx_ready, t - 2)
            act.activation(junk[t % 3], xst[t % 3][:, :], ACT.Square, accum_out=ssq_x[:, t:t + 1]).then_inc(ssqx_ready, 1)

        def h_hi(t):
            for b in range(2):
                act.wait_ge(xT_ready, 2 * t + b + 1)
                act.activation(hT_h[:, 4 * b:4 * b + 4, P * t:P * t + P],
                               ps[:, b, :].rearrange("p (k n) -> p k n", k=4), ACT.Copy).then_inc(hhi_ready, 1)

        def latent_stats(t):
            act.wait_ge(z_ready, t + 1)
            z = z_bank(t)
            unused = yrT[:, :, :].rearrange("p c n -> p (c n)")[:, (QR + KVR) * t:(QR + KVR) * (t + 1)]
            act.activation(unused[:, 0:QR], z[:, 0:QR], ACT.Square, accum_out=ssq_z[:, t, 0:1])
            act.activation(unused[:, QR:], z[:, QR:QR + KVR], ACT.Square, accum_out=ssq_z[:, t, 1:2])
            if t >= 2:
                act.wait_ge(latT_ready, t - 1)
            kr = krs[t % 2]
            act.activation(kr[:, 64:96], z[:, QR + KVR:LAT], ACT.Copy)
            act.activation(kr[:, 96:112], z[:, QR + KVR + 16:LAT], ACT.Copy)
            act.activation(kr[:, 112:128], z[:, QR + KVR:QR + KVR + 16], ACT.Copy).then_inc(zstat_ready, 1)

        def latents_hi(t):
            act.wait_ge(latT_ready, t + 1)
            act.activation(latT_h[:, :, P * t:P * t + P], ps[:, 2, 0:3 * P].rearrange("p (k n) -> p k n", k=3),
                           ACT.Copy).then_inc(lathi_ready, 1)

        square_x(0)
        split_latent_weights(0)
        h_hi(0)
        split_latent_weights(1)
        split_latent_weights(2)
        split_latent_weights(3)
        square_x(1)
        for i in range(1, NT + 3):
            if 2 <= i < NT:
                square_x(i)
            if 2 <= i <= NT:
                h_hi(i - 1)
            if 2 <= i <= NT + 1:
                latent_stats(i - 2)
            if 3 <= i:
                latents_hi(i - 3)

        def gate_sigmoid(c, g):
            dst, bias = ((ra, bias_a), (iu, bias_x))[g]
            for half in range(2):
                u = 4 * c + 2 * g + half
                act.wait_ge(gate_ready, u + 1)
                if c >= 1 and half == 0:
                    act.wait_ge(scan_done, c)
                act.activation(dst[:, HALF * half:HALF * half + HALF], ps[:, u % 4, :], ACT.Sigmoid,
                               bias=bias[:, c:c + 1]).then_inc(sig_ready, 1)

        def decay(c):
            act.wait_ge(sig_ready, 4 * c + 4)
            if c == 0:
                act.wait_ge(sp_ready, 1)
            if c >= 1:
                act.wait_ge(yr_done, c)
            act.activation(mh[:, :], ra[:, :], ACT.Exp, scale=sp16[:, c:c + 1]).then_inc(exp_ready, 1)
            act.activation(ra[:, :], ra[:, :], ACT.Exp, scale=sp8[:, c:c + 1]).then_inc(exp_ready, 1)
            act.wait_ge(min_ready, c + 1)
            act.activation(mh[:, :], mh[:, :], ACT.Sqrt, bias=1.0).then_inc(sqrt_ready, 1)

        def square_h(c):
            act.wait_ge(scan_done, c + 1)
            if c >= 2:
                act.wait_ge(hsq_summed, c - 1)
            act.activation(sq_sum[:, :] if c == 0 else hsq[:, :], mh[:, :], ACT.Square).then_inc(hsq_ready, 1)

        def chunk_out(c, halves=(0, 1)):
            kind, cc, _ = CHUNKS[c]
            for half in halves:
                m = z_use(c, half)
                act.wait_ge(z_ready, m + 1)
                if kind == "x":
                    if cc >= 1 and half == 0:
                        act.wait_ge(conv_done, cc)
                    if cc == 0 and half == 0:
                        act.wait_ge(latlo_ready, NT)
                    act.activation(xpad[:, 3 + HALF * half:3 + HALF * half + HALF], z_bank(m), ACT.Copy).then_inc(xpad_ready, 1)
                else:
                    u = 2 * (c - NC) + half
                    if u >= 2:
                        act.wait_ge(gate_done, u - 1)
                    act.activation(sg[u % 2][:, :], z_bank(m), ACT.Sigmoid).then_inc(sg_ready, 1)

        def misc_hi(step):
            i = misc_no[step]
            kind = step[0]
            bank = ps[:, misc_bank(i), :]
            if kind == "C":
                return
            act.wait_ge(misc_ready, i + 1)
            if kind == "V":
                _, half, part = step
                if half == 1:
                    act.wait_ge(pv_done, t_no[("T", 7, 2 * part + 1)] + 1)
                act.activation(vv[:, 2 * part:2 * part + 2, :, 0:VD],
                               bank.rearrange("p (j h d) -> p j h d", j=2, h=4), ACT.Copy).then_inc(mhi_ready, 1)
            elif kind == "K":
                _, pair, half = step
                if pair >= 2:
                    act.wait_ge(s_ready, s_no[("S", 2 * pair - 3, 7)] + 1)
                c = slice(HALF * half, HALF * half + HALF)
                act.activation(kh[0:64, 2 * (pair % 2), c], bank[0:64, :], ACT.Copy)
                act.activation(kh[0:64, 2 * (pair % 2) + 1, c], bank[64:128, :], ACT.Copy).then_inc(mhi_ready, 1)
            else:
                _, h, half = step
                if h >= 1:
                    act.wait_ge(s_ready, s_no[("S", h - 1, 4 * half + 3)] + 1)
                c = slice(HALF * half, HALF * half + HALF)
                u = 2 * h + half
                act.activation(qh[0:64, c], bank[0:64, :], ACT.Copy).then_inc(mhi_ready, 1)
                if u >= 2:
                    act.wait_ge(q_ready, u - 1)
                act.activation(qc[u % 2][64:128, :], bank[64:128, :], ACT.Copy).then_inc(qc_ready, 1)

        def exponentials(h, t):
            k = s_no[("S", h, t)]
            act.wait_ge(max_ready, k + 1)
            if h >= 1:
                act.wait_ge(pt_ready, t_no[("T", 2 * (h - 1) + t // 4, t)] + 1)
            act.activation(probs[t][:, :], tile_scores(t), ACT.Exp, bias=nmax[:, NT * h + t:NT * h + t + 1],
                           accum_out=rsum[:, NT * h + t:NT * h + t + 1]).then_inc(p_ready, 1)

        def probs_hi(n, j):
            u = t_no[("T", n, j)]
            act.wait_ge(pt_ready, u + 1)
            if u >= 3:
                act.wait_ge(pv_done, u - 2)
            c0 = P * query_tiles(n, j)
            act.activation(pth[u % 3][:, c0:HALF], ps[:, 4 + u % 2, c0:HALF], ACT.Copy).then_inc(pthi_ready, 1)

        def copy_y(n):
            act.wait_ge(pv_done, t_no[("T", n, 4 * (n % 2) + 3)] + 1)
            if n >= 1:
                act.wait_ge(misc_ready, misc_no[("C", n - 1)] + 1)
            act.activation(yTs[:, :], ps[:, 6, :], ACT.Copy).then_inc(yT_copied, 1)

        for c in range(len(CHUNKS)):
            if 4 <= c < 4 + NC:
                gate_sigmoid(c - 4, 0)
                gate_sigmoid(c - 4, 1)
            if c == 1:
                act.wait_ge(sp_in, 1)
                act.activation(sp[:, 2, :], sp[:, 1, :], ACT.Exp, scale=-1.0).then_inc(lru_exp, 1)
            if c < len(CHUNKS) - 1:
                chunk_out(c)
            if 5 <= c < 5 + NC:
                square_h(c - 5)
            if 4 <= c < 4 + NC:
                decay(c - 4)
        chunk_out(len(CHUNKS) - 1, (0,))
        act.wait_ge(yr_done, NC)
        misc_hi(steps[0])
        misc_hi(steps[1])
        act.wait_ge(ssr_ready, 1)
        act.activation(kr_h[64:96, :], kpe[64:96, :], ACT.Copy).then_inc(krope_hi, 1)
        act.wait_ge(krope_hi, 1)
        chunk_out(len(CHUNKS) - 1, (1,))
        misc_hi(steps[2])
        act.activation(kh[64:96, 0, :], f32(kr_h[64:96, :]), ACT.Copy).then_inc(krope_hi, 1)

        for step in scores_after_transposes(steps)[3:]:
            if step[0] in "VKQC":
                misc_hi(step)
            elif step[0] == "S":
                exponentials(*step[1:])
            elif step[0] == "W":
                w = step[1]
                use = USE_WR + w
                s, v = raw_landed(use)
                act.wait_ge(s, v)
                act.wait_ge(misc_ready, misc_no[("Q", H - 1, 1)] + 1)
                act.wait_ge(q_ready, 2 * H)
                if w >= NC:
                    act.wait_ge(s_ready, s_no[("S", H - 1, NT - 1)] + 1)
                act.activation((wr_h + wm_h)[w][:, :], raw[use % 2][:, :], ACT.Copy).then_inc(w_act_hi, 1)
            elif step[0] == "T":
                probs_hi(*step[1:])
            elif step[0] == "Y":
                copy_y(*step[1:])

        def square_y(t):
            act.wait_ge(misc_done, len(MISC))
            if t >= 2:
                act.wait_ge(ssm_ready, t - 1)
            unused = trig[:, HALF * (t % 2):HALF * (t % 2) + HALF]
            act.activation(unused, ynat[:, t, :], ACT.Square, accum_out=ssq_m[:, t:t + 1]).then_inc(ssm_ready, 1)

        def y_hi(t):
            act.wait_ge(ymf_ready, t + 1)
            if t >= 2:
                act.wait_ge(m_ready, t - 1)
            act.activation(ym_h[t % 2][:, :, :], ymf[:, :, :], ACT.Copy).then_inc(ymhi_ready, 1)

        act.wait_ge(pt_ready, len(t_no))
        act.wait_ge(pv_done, len(t_no))
        y_hi(0)
        for t in range(4):
            square_y(t)

        def square_out(t):
            if t >= 3:
                act.wait_ge(sso_ready, t - 2)
            for n, c in enumerate(out_columns(t)):
                act.wait_ge(m_added, t + 1 + n)
                act.activation(unused_sq[t % 3][:, c], xres[t % 4][:, c], ACT.Square,
                               accum_out=ssq_o[:, t + n:t + n + 1]).then_inc(sso_ready, 1)

        for t in range(1, NT):
            y_hi(t)
            if t + 3 < NT:
                square_y(t + 3)
            if t >= 2:
                square_out(t - 2)
        square_out(NT - 2)
        square_out(NT - 1)

    @block.vector
    def _(dve):
        own = [0]

        def after(ins):
            own[0] += 1
            ins.then_inc(dve_own, 1)
            dve.wait_ge(dve_own, own[0])

        def split_latent_weights(k):
            dve.wait_ge(latw_hi, k + 1)
            dve.tensor_tensor(lat_w_l[:, 2 * k:2 * k + 2, :], lat_raw[k][:, :, :], f32(lat_w_h[:, 2 * k:2 * k + 2, :]),
                              ALU.subtract).then_inc(latw_lo, 1)

        def normalise_x(t):
            dve.wait_ge(rstdx_ready, t + 1)
            x = xst[t % 3]
            dve.scalar_tensor_tensor(x[:, :], x[:, :], rstd_x[:, t:t + 1], g_in_row[:, :], ALU.mult, ALU.mult)\
               .then_inc(h_ready, 1)

        def h_lo(t):
            for b in range(2):
                dve.wait_ge(hhi_ready, 2 * t + b + 1)
                dve.tensor_tensor(hT_l[:, 4 * b:4 * b + 4, P * t:P * t + P], ps[:, b, :].rearrange("p (k n) -> p k n", k=4),
                                  f32(hT_h[:, 4 * b:4 * b + 4, P * t:P * t + P]), ALU.subtract).then_inc(hlo_ready, 1)

        def normalise_latents(t):
            dve.wait_ge(rstdz_ready, t + 1)
            if t >= 2:
                dve.wait_ge(latT_ready, t - 1)
            z = z_bank(t)
            dve.scalar_tensor_tensor(latn[t % 2][:, 0:QR], z[:, 0:QR], rstd_z[:, t, 0:1], g_lat_row[:, 0:QR], ALU.mult, ALU.mult)
            dve.scalar_tensor_tensor(latn[t % 2][:, QR:], z[:, QR:QR + KVR], rstd_z[:, t, 1:2], g_lat_row[:, QR:],
                                     ALU.mult, ALU.mult).then_inc(latn_ready, 1)

        def latents_lo(t):
            c = slice(P * t, P * t + P)
            dve.wait_ge(lathi_ready, t + 1)
            dve.tensor_tensor(latT_l[:, :, c], ps[:, 2, 0:3 * P].rearrange("p (k n) -> p k n", k=3),
                              f32(latT_h[:, :, c]), ALU.subtract)
            kr = ps[:, 2, 3 * P:4 * P]
            dve.tensor_tensor(rope_t[64:96, :], kr[96:128, :], trig[96:128, c], ALU.mult)
            dve.tensor_tensor(kpe[64:96, c], kr[64:96, :], trig[64:96, c], ALU.mult).then_inc(kpe_half, 1)
            dve.wait_ge(kpe_half, t + 1)
            dve.tensor_tensor(kpe[64:96, c], kpe[64:96, c], rope_t[64:96, :], ALU.add).then_inc(latlo_ready, 1)

        def softplus_start():
            after(dve.tensor_scalar(sp[:, 0, :], lru[:, :], -1.0, None, ALU.mult))
            dve.tensor_tensor(sp[:, 1, :], lru[:, :], sp[:, 0, :], ALU.max).then_inc(sp_in, 1)

        def softplus_end():
            e, w, w2, s = sp[:, 2, :], sp[:, 3, :], sp[:, 4, :], sp[:, 5, :]
            dve.wait_ge(lru_exp, 1)
            after(dve.tensor_scalar(sp[:, 6, :], e, 2.0, None, ALU.add))
            after(dve.reciprocal(sp[:, 7, :], sp[:, 6, :]))
            after(dve.tensor_tensor(w, e, sp[:, 7, :], ALU.mult))
            after(dve.tensor_tensor(w2, w, w, ALU.mult))
            after(dve.tensor_scalar(s, w2, 1.0 / 17.0, None, ALU.mult))
            for n in (15.0, 13.0, 11.0, 9.0, 7.0, 5.0, 3.0):
                after(dve.scalar_tensor_tensor(s, s, 1.0 / n, w2, ALU.add, ALU.mult))
            after(dve.scalar_tensor_tensor(s, s, 1.0, w, ALU.add, ALU.mult))
            after(dve.tensor_scalar(sp[:, 8, :], sp[:, 0, :], 0.0, None, ALU.max))
            after(dve.scalar_tensor_tensor(sp[:, 9, :], s, 2.0, sp[:, 8, :], ALU.mult, ALU.add))
            after(dve.tensor_scalar(sp8[:, :], sp[:, 9, :], -8.0, None, ALU.mult))
            dve.tensor_scalar(sp16[:, :], sp[:, 9, :], -16.0, None, ALU.mult).then_inc(sp_ready, 1)

        dve.memset(one_col[:, :], 1.0)
        dve.memset(half_rows[:, :], 0.0)
        after(dve.memset(masked[:, :], MASKED))
        dve.memset(half_rows[:, 0:64], 1.0)
        dve.memset(krs[0][:, :], 0.0)
        after(dve.memset(krs[1][:, :], 0.0))
        dve.wait_ge(first_in, 16)
        normalise_x(0)
        split_latent_weights(0)
        h_lo(0)
        split_latent_weights(1)
        split_latent_weights(2)
        split_latent_weights(3)
        normalise_x(1)
        for i in range(1, NT + 3):
            if 2 <= i < NT:
                normalise_x(i)
            if 2 <= i <= NT:
                h_lo(i - 1)
            if i == 2:
                dve.wait_ge(const_in, 16 * N_CONST)
                after(dve.tensor_scalar(g_lat_row[:, 0:QR], g_lat_row[:, 0:QR], SCALE, None, ALU.mult))
            if 2 <= i <= NT + 1:
                normalise_latents(i - 2)
            if 3 <= i:
                latents_lo(i - 3)

        def convolve(c):
            dve.wait_ge(xpad_ready, 2 * c + 2)
            if c == 1:
                dve.wait_ge(gw_ready, 1)
            y = xr[c]
            after(dve.tensor_scalar(y, xpad[:, 3:3 + SEQ], conv_w[:, 3, c:c + 1], conv_b[:, c:c + 1], ALU.mult, ALU.add))
            for k in range(2, 0, -1):
                after(dve.scalar_tensor_tensor(y, xpad[:, k:k + SEQ], conv_w[:, k, c:c + 1], y, ALU.mult, ALU.add))
            dve.scalar_tensor_tensor(y, xpad[:, 0:SEQ], conv_w[:, 0, c:c + 1], y, ALU.mult, ALU.add).then_inc(conv_done, 1)

        def gated_input(c):
            dve.wait_ge(sig_ready, 4 * c + 4)
            dve.wait_ge(conv_done, c + 1)
            dve.tensor_tensor(iu[:, :], iu[:, :], xr[c], ALU.mult)
            dve.wait_ge(exp_ready, 2 * c + 1)
            dve.tensor_scalar(mh[:, :], mh[:, :], 1.0, -1.0, ALU.min, ALU.mult).then_inc(min_ready, 1)

        def recur(c):
            dve.wait_ge(sqrt_ready, c + 1)
            after(dve.memset(mh[:, 0:1], 1.0))
            after(dve.scalar_tensor_tensor(iu[:, :], mh[:, :], 1e-6, iu[:, :], ALU.max, ALU.mult))
            dve.wait_ge(exp_ready, 2 * c + 2)
            dve.tensor_tensor_scan(mh[:, :], ra[:, :], iu[:, :], 0.0, ALU.mult, ALU.add).then_inc(scan_done, 1)

        def gate_out(c, halves=(0, 1)):
            kind, cc, _ = CHUNKS[c]
            dst, gain = (yrT, g_rnn) if kind == "gr" else (gmT, g_mla)
            for half in halves:
                u = 2 * (c - NC) + half
                dve.wait_ge(sg_ready, u + 1)
                dve.scalar_tensor_tensor(dst[:, cc, HALF * half:HALF * half + HALF], z_bank(z_use(c, half)),
                                         gain[:, cc:cc + 1], sg[u % 2][:, :], ALU.mult, ALU.mult).then_inc(gate_done, 1)

        def gate_h(c):
            dve.wait_ge(scan_done, c + 1)
            dve.wait_ge(hsq_ready, c + 1)
            dve.wait_ge(gate_done, 2 * c + 2)
            dve.tensor_tensor(yrT[:, c, :], yrT[:, c, :], mh[:, :], ALU.mult).then_inc(yr_done, 1)

        def misc_lo(step):
            i = misc_no[step]
            kind = step[0]
            bank = ps[:, misc_bank(i), :]
            if kind == "C":
                _, n = step
                h, g = divmod(n, 2)
                r = slice(NT * h + 4 * g, NT * h + 4 * g + 4)
                dve.wait_ge(p_ready, s_no[("S", h, 4 * g + 3)] + 1)
                after(dve.reciprocal(rinv[:, r], rsum[:, r]))
                dve.wait_ge(misc_ready, i + 1)
                dve.tensor_tensor(ynat[:, 4 * g:4 * g + 4, VD * h:VD * h + VD],
                                  bank[:, 0:4 * VD].rearrange("p (t d) -> p t d", t=4),
                                  rinv[:, r].rearrange("p (t o) -> p t o", o=1).to_broadcast((P, 4, VD)), ALU.mult)\
                   .then_inc(misc_done, 1)
                return
            dve.wait_ge(mhi_ready, i + 1 - sum(s[0] == "C" for s in MISC[:i]))
            if kind == "V":
                _, half, part = step
                j = slice(2 * part, 2 * part + 2)
                dve.tensor_tensor(vv[:, j, :, VD:P], bank.rearrange("p (j h d) -> p j h d", j=2, h=4),
                                  f32(vv[:, j, :, 0:VD]), ALU.subtract).then_inc(misc_done, 1)
            elif kind == "K":
                _, pair, half = step
                c = slice(HALF * half, HALF * half + HALF)
                b = 2 * (pair % 2)
                dve.tensor_tensor(kl[0:64, b, c], bank[0:64, :], f32(kh[0:64, b, c]), ALU.subtract)
                dve.tensor_tensor(kl[0:64, b + 1, c], bank[64:128, :], f32(kh[0:64, b + 1, c]), ALU.subtract).then_inc(misc_done, 1)
            else:
                _, h, half = step
                c = slice(HALF * half, HALF * half + HALF)
                dve.tensor_tensor(ql[0:64, c], bank[0:64, :], f32(qh[0:64, c]), ALU.subtract).then_inc(misc_done, 1)

        def row_max(h, t):
            k = s_no[("S", h, t)]
            i = NT * h + t
            dve.wait_ge(s_ready, k + 1)
            dve.tensor_reduce(nmax[:, i:i + 1], tile_scores(t), AX.X, ALU.max, negate=True).then_inc(max_ready, 1)

        def probs_lo(n, j):
            u = t_no[("T", n, j)]
            dve.wait_ge(pthi_ready, u + 1)
            c0 = P * query_tiles(n, j)
            dve.tensor_tensor(ptl[u % 3][:, c0:HALF], ps[:, 4 + u % 2, c0:HALF], f32(pth[u % 3][:, c0:HALF]), ALU.subtract)\
               .then_inc(ptlo_ready, 1)

        for c in range(len(CHUNKS)):
            if c == 0:
                softplus_start()
                dve.wait_ge(z_ready, NT)
                after(dve.memset(xpad[:, 0:3], 0.0))
            if c == 2:
                softplus_end()
            if c < NC:
                convolve(c)
            elif c < len(CHUNKS) - 1:
                gate_out(c)
            if 5 <= c < 5 + NC:
                gate_h(c - 5)
            if 4 <= c < 4 + NC:
                gated_input(c - 4)
                recur(c - 4)
        gate_out(len(CHUNKS) - 1, (0,))
        dve.wait_ge(ssr_ready, 1)
        dve.tensor_copy(ssq_r[:, :], ps[:, 0, 0:NT]).then_inc(ssr_copied, 1)
        misc_lo(steps[0])
        misc_lo(steps[1])
        dve.wait_ge(krope_hi, 1)
        after(dve.tensor_tensor(kr_l[64:96, :], kpe[64:96, :], f32(kr_h[64:96, :]), ALU.subtract))
        dve.wait_ge(z_ready, NT + 2 * len(CHUNKS))
        dve.tensor_copy(kl[64:96, 0, :], f32(kr_l[64:96, :])).then_inc(krope_ready, 1)
        gate_out(len(CHUNKS) - 1, (1,))
        misc_lo(steps[2])

        for step in steps[3:]:
            if step[0] in "VKQC":
                misc_lo(step)
            elif step[0] == "S":
                row_max(*step[1:])
            elif step[0] == "W":
                w = step[1]
                dve.wait_ge(w_act_hi, OUT_W.index(w) + 1)
                u = (USE_WR + w) % 2
                dve.tensor_tensor((wr_l + wm_l)[w][:, :], raw[u][:, :], f32((wr_h + wm_h)[w][:, :]), ALU.subtract)\
                   .then_inc(raw_split[u], 1)
            elif step[0] == "T":
                probs_lo(*step[1:])

        def y_gate(t):
            dve.wait_ge(ymT_ready, t + 1)
            if t >= 1:
                dve.wait_ge(ymlo_ready, t)
            dve.tensor_tensor(ymf[:, :, :], ps[:, 6 + t % 2, :].rearrange("p (c n) -> p c n", c=NC),
                              gmT[:, :, P * t:P * t + P], ALU.mult).then_inc(ymf_ready, 1)

        def y_lo(t):
            dve.wait_ge(ymhi_ready, t + 1)
            dve.tensor_tensor(ym_l[t % 2][:, :, :], ymf[:, :, :], f32(ym_h[t % 2][:, :, :]), ALU.subtract).then_inc(ymlo_ready, 1)

        def add_r(t):
            dve.wait_ge(r_ready, t + 1)
            dve.wait_ge(rstdr_ready, 1)
            dve.wait_ge(res_in[t % 4], 16 * (t // 4 + 1))
            dve.scalar_tensor_tensor(xres[t % 4][:, :], out_banks("R", t), rstd_r[:, t:t + 1],
                                     xres[t % 4][:, :], ALU.mult, ALU.add).then_inc(r_added, 1)

        def add_m(t):
            dve.wait_ge(rstdm_ready, t + 1)
            dve.wait_ge(r_added, t + 1)
            for n, c in enumerate(out_columns(t)):
                dve.wait_ge(m_ready, t + 1 + n)
                dve.scalar_tensor_tensor(xres[t % 4][:, c], out_banks("M", t)[:, c], rstd_m[:, t:t + 1],
                                         xres[t % 4][:, c], ALU.mult, ALU.add).then_inc(m_added, 1)

        def finish(t):
            dve.wait_ge(rstdo_ready, t + 1)
            if t == 0:
                dve.wait_ge(fg_in, 16)
            if t >= 2:
                dve.wait_ge(out_done[t % 2], 16 * (t // 2))
            for c in out_columns(t):
                dve.scalar_tensor_tensor(ost[t % 2][:, c], xres[t % 4][:, c], rstd_o[:, t:t + 1], fg_row[:, c],
                                         ALU.mult, ALU.mult).then_inc(o_ready, 1)

        y_gate(0)
        y_lo(0)
        add_r(0)
        for t in range(NT):
            if t + 1 < NT:
                y_gate(t + 1)
                y_lo(t + 1)
                add_r(t + 1)
            if t >= 1:
                finish(t - 1)
            add_m(t)
        finish(NT - 1)

    @block.gpsimd
    def _(pool):
        own = [0]

        def after(ins):
            own[0] += 1
            ins.then_inc(pool_own, 1)
            pool.wait_ge(pool_own, own[0])

        def rstd(dst, ssq, n, scale, ready):
            if scale is None:
                after(pool.tensor_tensor(dst, ssq, inv_n[:, :], ALU.mult))
                after(pool.tensor_scalar(dst, dst, 1.0, EPS, ALU.mult, ALU.add))
            else:
                after(pool.tensor_scalar(dst, ssq, scale, EPS, ALU.mult, ALU.add))
            pool.tensor_tensor(dst, dst, minus_half[:, 0:n], ALU.pow).then_inc(ready, 1)

        def split(hi, lo, src, hi_sem, count):
            pool.tensor_scalar(hi, src, 1.0, 0.0, ALU.mult, ALU.add).then_inc(hi_sem, 1)
            pool.wait_ge(hi_sem, count)
            return pool.tensor_tensor(lo, src, f32(hi), ALU.subtract)

        def split_chunk(c):
            use = USE_CHUNK + c
            s, v = raw_landed(use)
            pool.wait_ge(s, v)
            if c >= 2:
                pool.wait_ge(z_ready, z_use(c - 2, 1) + 1)
            elif c == 0:
                pool.wait_ge(latw_lo, 4)
            src = raw[use % 2][:, :].rearrange("p (k n) -> p k n", k=KD)
            split(cw_h[c % 2][:, :, :], cw_l[c % 2][:, :, :], src, cw_hi, c + 1).then_inc(raw_split[use % 2], 1)

        def rstd_x_of(t):
            pool.wait_ge(ssqx_ready, t + 1)
            rstd(rstd_x[:, t:t + 1], ssq_x[:, t:t + 1], 1, 1.0 / D, rstdx_ready)

        def rstd_z_of(t):
            pool.wait_ge(zstat_ready, t + 1)
            rstd(rstd_z[:, t, :], ssq_z[:, t, :], 2, None, rstdz_ready)

        pool.memset(gate_raw[:, :, :, :], 0.0).then_inc(zeroed, 1)
        pool.memset(inv_n[:, 0:1], 1.0 / QR)
        pool.memset(inv_n[:, 1:2], 1.0 / KVR)
        after(pool.memset(minus_half[:, :], -0.5))
        for i in range(NT + 2):
            if i < NT:
                rstd_x_of(i)
            if i == 5:
                split_chunk(0)
            if i == 7:
                split_chunk(1)
            if 2 <= i:
                rstd_z_of(i - 2)
        pool.wait_ge(latlo_ready, NT)
        pool.wait_ge(gates_in, 64)
        split(gw_h[:, :, :, :], gw_l[:, :, :, :], gate_raw, gw_hi, 1).then_inc(gw_ready, 1)

        def split_xr(c):
            pool.wait_ge(conv_done, c + 1)
            if c >= 1:
                pool.wait_ge(gate_ready, 4 * c)
            split(xr_h[:, :], xr_l[:, :], xr[c], xr_hi_done, c + 1).then_inc(xrs_ready, 1)

        def sum_squares(c):
            pool.wait_ge(hsq_ready, c + 1)
            if c >= 2:
                pool.wait_ge(hsq_summed, c - 1)
            pool.tensor_tensor(sq_sum[:, :], sq_sum[:, :], hsq[:, :], ALU.add).then_inc(hsq_summed, 1)

        for c in range(len(CHUNKS)):
            if c + 2 < len(CHUNKS):
                split_chunk(c + 2)
            if 1 <= c < 1 + NC:
                split_xr(c - 1)
            if 6 <= c < 5 + NC:
                sum_squares(c - 5)
        pool.wait_ge(yr_done, NC)
        for k in range(3):
            use = USE_Q + k
            s, v = raw_landed(use)
            pool.wait_ge(s, v)
            if k < 2:
                hi, lo = wq_h[:, k, :, :], wq_l[:, k, :, :]
            else:
                hi, lo = wkv_h[:, :], wkv_l[:, :]
            src = raw[use % 2][:, :]
            if k < 2:
                src = src.rearrange("p (h n) -> p h n", h=H)
            split(hi, lo, src, aw_hi, k + 1).then_inc(raw_split[use % 2], 1)
        pool.wait_ge(ssr_copied, 1)
        rstd(rstd_r[:, :], ssq_r[:, :], NT, 1.0 / RNN, rstdr_ready)

        def split_yr(c):
            if c in (0, 2):
                pool.wait_ge(q_ready, 2 * H - (2 if c == 0 else 0))
            pool.wait_ge(s_ready, s_no[("S", 5, 7)] + 1)
            split(yr_h[c][:, :], yr_l[c][:, :], yrT[:, c, :], yr_hi_done, c + 1).then_inc(yr_lo, 1)

        def split_out(use, hi, lo, count):
            s, v = raw_landed(use)
            pool.wait_ge(s, v)
            split(hi[:, :], lo[:, :], raw[use % 2][:, :], w_out_hi, count).then_inc(raw_split[use % 2], 1)

        pool.wait_ge(rstdr_ready, 1)
        for h in range(H):
            for half in range(2):
                u = 2 * h + half
                c = slice(HALF * half, HALF * half + HALF)
                if u >= 1:
                    pool.wait_ge(q_ready, u)
                if u == 2:
                    pool.wait_ge(krope_copied, 6)
                pool.wait_ge(qc_ready, u + 1)
                s = qc[u % 2]
                after(pool.tensor_tensor(qn[64:96, :], s[96:128, :], trig[96:128, c], ALU.mult))
                after(pool.tensor_tensor(s[64:96, :], s[64:96, :], trig[64:96, c], ALU.mult))
                after(pool.tensor_tensor(qn[64:96, :], qn[64:96, :], s[64:96, :], ALU.add))
                if h >= 1:
                    pool.wait_ge(s_ready, s_no[("S", h - 1, 4 * half + 3)] + 1)
                split(qh[64:96, c], ql[64:96, c], qn[64:96, :], qrope_hi, u + 1).then_inc(q_ready, 1)
            if h == 0:
                pool.wait_ge(krope_hi, 2)
                pool.wait_ge(krope_ready, 1)
                pool.wait_ge(q_ready, 2)
                for i in range(1, 4):
                    for kk in (kh, kl):
                        pool.tensor_scalar(kk[64:96, i, :], f32(kk[64:96, 0, :]), 1.0, 0.0, ALU.mult, ALU.add)\
                            .then_inc(krope_copied, 1)
            if h == H - 2:
                split_yr(0)
                split_yr(1)
                pool.wait_ge(yr_lo, 2)
        split_yr(2)
        split_yr(3)
        pool.wait_ge(misc_ready, misc_no[("Q", H - 1, 1)] + 1)
        for n, w in enumerate(w for w in range(2 * NC) if w not in OUT_W):
            if w >= NC:
                pool.wait_ge(s_ready, s_no[("S", H - 1, NT - 1)] + 1)
            split_out(USE_WR + w, (wr_h + wm_h)[w], (wr_l + wm_l)[w], n + 1)
        for t in range(NT):
            pool.wait_ge(ssm_ready, t + 1)
            rstd(rstd_m[:, t:t + 1], ssq_m[:, t:t + 1], 1, 1.0 / (H * VD), rstdm_ready)
            if t >= 4:
                pool.wait_ge(sso_ready, t - 3)
                rstd(rstd_o[:, t - 4:t - 3], ssq_o[:, t - 4:t - 3], 1, 1.0 / D, rstdo_ready)
        for t in range(NT - 4, NT):
            pool.wait_ge(sso_ready, t + len(out_columns(t)))
            if t == NT - 1:
                after(pool.tensor_tensor(ssq_o[:, t:t + 1], ssq_o[:, t:t + 1], ssq_o[:, NT:NT + 1], ALU.add))
            rstd(rstd_o[:, t:t + 1], ssq_o[:, t:t + 1], 1, 1.0 / D, rstdo_ready)

    ctx.close()


_INS = ["x", "norm_in_g", "w_in", "q_norm_g", "w_q_b", "kv_norm_g", "w_kv_b", "conv_w", "conv_b", "w_rg_a",
        "b_rg_a", "w_rg_x", "b_rg_x", "lru_param", "out_norm_mla_g", "out_norm_rnn_g", "w_out", "final_norm_g"]


def _constants():
    import numpy as np

    eye = np.eye(P, dtype=np.float32)
    pos = np.arange(SEQ, dtype=np.float32)
    inv_freq = np.float32(10000.0) ** (-np.arange(0, ROPE, 2, dtype=np.float32) / np.float32(ROPE))
    ang = (pos[:, None] * inv_freq[None, :].astype(np.float32)).astype(np.float32)
    cos, sin = np.cos(ang).T, np.sin(ang).T
    trig = np.concatenate([cos, cos, -sin, sin]).astype(np.float32)
    return {"ident": eye, "stack": np.concatenate([eye[:VD, :VD], eye[:VD, :VD]]), "trig": trig}


def kernel(**inputs):
    import numpy as _np
    import concourse.bacc as _bacc
    from concourse import mybir as _mybir
    from concourse.bass_utils import run_bass_kernel_spmd as _run

    nc = _bacc.Bacc("TRN2", target_bir_lowering=False, num_devices=1)
    arrays, args = {}, {}
    for name, value in [(n, inputs[n]) for n in _INS] + list(_constants().items()):
        v = _np.ascontiguousarray(value)
        arrays[f"in_{name}_dram"] = v
        args[name] = nc.dram_tensor(f"in_{name}_dram", v.shape, _mybir.dt.from_np(v.dtype), kind="ExternalInput").ap()
    out = nc.dram_tensor("out_0_dram", (1, SEQ, D), _mybir.dt.float32, kind="ExternalOutput").ap()
    build(nc, args, out)
    r = _run(nc, [arrays], core_ids=[0])
    return r.results[0]["out_0_dram"]
```
